# Optimizing a Trainium2 kernel written in Bass

```python
import math
import jax, jax.numpy as jnp
from jax import lax
import numpy as np

D_MODEL = 1024
BATCH = 1
SEQ = 1024
DEPTH = 1
DEC_BATCH = 8
DEC_SEQ = 4
PAST_LEN = 4096
PAGE_SIZE = 128

MIX_ATTN = D_MODEL // 2
N_HEADS = 8
HEAD_DIM = MIX_ATTN // N_HEADS
N_KV_HEADS = 2
GROUP = N_HEADS // N_KV_HEADS
CONV_CH = D_MODEL - MIX_ATTN
CONV_W = 31
CMP_BLOCK = 32
CMP_STRIDE = 16
CMP_HID = 2 * HEAD_DIM
SLC_BLOCK = 64
TOP_K = 16
WINDOW = 512
Q_BLOCK = 128
D_FF = 4 * D_MODEL
PLE_DIM = 256
Q_COLS = N_HEADS * HEAD_DIM
KV_COLS = 2 * N_KV_HEADS * HEAD_DIM
GATE_COLS = 3 * N_HEADS
CONV_COLS = 2 * CONV_CH
N_IN = Q_COLS + 3 * KV_COLS + GATE_COLS + CONV_COLS
EPS = 1e-6
NEG = -1e30
FORCE_BONUS = 1e4

kernel_name = "nsa_conformer_parallel_heads_step"

F32 = jnp.float32

def rmsnorm(x, g):
    xf = x.astype(F32)
    y = xf * lax.rsqrt(jnp.mean(xf * xf, -1, keepdims=True) + EPS)
    return (y * g.astype(F32)).astype(x.dtype)

def layernorm(x, g, b):
    xf = x.astype(F32)
    mu = jnp.mean(xf, -1, keepdims=True)
    xc = xf - mu
    y = xc * lax.rsqrt(jnp.mean(xc * xc, -1, keepdims=True) + EPS)
    return (y * g.astype(F32) + b.astype(F32)).astype(x.dtype)

def alibi_slopes():
    s = 2.0 ** (-8.0 * np.arange(1, N_HEADS + 1) / N_HEADS)
    return jnp.asarray(s, F32).reshape(N_KV_HEADS, GROUP)

def masked_softmax(s, mask):
    s = jnp.where(mask, s, NEG)
    e = jnp.where(mask, jnp.exp(s - jnp.max(s, -1, keepdims=True)), 0.0)
    return e / jnp.maximum(jnp.sum(e, -1, keepdims=True), 1e-30)

def compress(kv, w1, w2, pe):
    B, T = kv.shape[:2]
    n_chunk = T // CMP_STRIDE
    c = kv[:, :n_chunk * CMP_STRIDE].reshape(B, n_chunk, CMP_STRIDE, 2, N_KV_HEADS, HEAD_DIM).astype(F32)
    lo = jnp.einsum('bnjchd,cjde->bnche', c, w1[:, :CMP_STRIDE])
    hi = jnp.einsum('bnjchd,cjde->bnche', c, w1[:, CMP_STRIDE:])
    pe_term = jnp.einsum('cjd,cjde->ce', pe, w1)
    pre = lo[:, :-1] + hi[:, 1:] + pe_term[:, None, :]
    return jnp.einsum('bnche,ced->bnchd', jax.nn.gelu(pre), w2).astype(F32)

def nsa_core(q, qpos, gates, cmp_kv, fetch, n_sel, win_kv, win_pos):
    B, Tq = q.shape[:2]
    slopes = alibi_slopes()[:, :, None, None]
    qg = q.reshape(B, Tq, N_KV_HEADS, GROUP, HEAD_DIM).astype(F32) * (HEAD_DIM ** -0.5)

    n_cmp = cmp_kv.shape[1]
    cmp_end = jnp.arange(n_cmp) * CMP_STRIDE + (CMP_BLOCK - 1)
    d_c = qpos[:, None] - cmp_end[None, :]
    s = jnp.einsum('btkgd,bnkd->bkgtn', qg, cmp_kv[:, :, 0]) - slopes * d_c.astype(F32)
    p_cmp = masked_softmax(s, d_c >= 0)
    o_cmp = jnp.einsum('bkgtn,bnkd->btkgd', p_cmp, cmp_kv[:, :, 1])

    ci = jnp.arange(n_cmp)[:, None] * CMP_STRIDE
    sj = jnp.arange(n_sel)[None, :] * SLC_BLOCK
    cover = ((ci + CMP_BLOCK > sj) & (ci < sj + SLC_BLOCK)).astype(F32)
    imp = jnp.einsum('bkgtn,nj->bktj', p_cmp, cover)
    jj = jnp.arange(n_sel)[None, :]
    cur = (qpos // SLC_BLOCK)[:, None]
    forced = (jj == 0) | (jj == cur) | (jj == cur - 1)
    score = jnp.where(jj * SLC_BLOCK <= qpos[:, None], imp, -1.0) + jnp.where(forced, FORCE_BONUS, 0.0)
    _, idx = lax.top_k(score, min(TOP_K, n_sel))
    sel = fetch(idx)
    kpos = idx[..., None] * SLC_BLOCK + jnp.arange(SLC_BLOCK)
    d_s = (qpos[:, None, None] - kpos).reshape(B, N_KV_HEADS, 1, Tq, -1)
    ksel = sel[..., 0, :].reshape(B, N_KV_HEADS, Tq, -1, HEAD_DIM).astype(F32)
    vsel = sel[..., 1, :].reshape(B, N_KV_HEADS, Tq, -1, HEAD_DIM).astype(F32)
    s = jnp.einsum('btkgd,bktmd->bkgtm', qg, ksel) - slopes * d_s.astype(F32)
    p = masked_softmax(s, d_s >= 0)
    o_slc = jnp.einsum('bkgtm,bktmd->btkgd', p, vsel)

    d_w = qpos[:, None] - win_pos[None, :]
    mask_w = (d_w >= 0) & (d_w < WINDOW) & (win_pos[None, :] >= 0)
    s = jnp.einsum('btkgd,bskd->bkgts', qg, win_kv[:, :, 0].astype(F32)) - slopes * d_w.astype(F32)
    p = masked_softmax(s, mask_w)
    o_win = jnp.einsum('bkgts,bskd->btkgd', p, win_kv[:, :, 1].astype(F32))

    g = gates.reshape(B, Tq, 3, N_KV_HEADS, GROUP, 1)
    o = g[:, :, 0] * o_cmp + g[:, :, 1] * o_slc + g[:, :, 2] * o_win
    return o.reshape(B, Tq, MIX_ATTN).astype(q.dtype)

def mixer_inputs(x, g, w_in):
    B, T = x.shape[:2]
    proj = rmsnorm(x, g) @ w_in
    cuts = [int(c) for c in np.cumsum([Q_COLS, KV_COLS, KV_COLS, KV_COLS, GATE_COLS])]
    q, kc, ks, kw, gt, cv = jnp.split(proj, cuts, axis=-1)
    kv = lambda a: a.reshape(B, T, 2, N_KV_HEADS, HEAD_DIM)
    gates = jax.nn.sigmoid(gt.astype(F32)).reshape(B, T, 3, N_HEADS)
    a, b = jnp.split(cv, 2, axis=-1)
    u = a * jax.nn.sigmoid(b)
    return q.reshape(B, T, N_HEADS, HEAD_DIM), kv(kc), kv(ks), kv(kw), gates, u

def conv_tail(hist, conv_w, conv_b, ln_g, ln_b):
    y = lax.conv_general_dilated(hist, conv_w[:, None, :].astype(hist.dtype), (1,), 'VALID',
                                 dimension_numbers=('NWC', 'WIO', 'NWC'),
                                 feature_group_count=CONV_CH) + conv_b
    y = layernorm(y, ln_g, ln_b)
    return y * jax.nn.sigmoid(y)

def layer_tail(x, mix, w_out, g_mlp, w_up, w_down, g_ple, w_ple, w_ple_gate, p):
    x = x + mix @ w_out
    x = x + jnp.square(jax.nn.relu(rmsnorm(x, g_mlp) @ w_up)) @ w_down
    x = x + (p @ w_ple) * jax.nn.sigmoid(rmsnorm(x, g_ple) @ w_ple_gate)
    return x

def nsa_prompt(q, kv_cmp, kv_slc, kv_win, gates, w1, w2, pe):
    B, T = q.shape[:2]
    cmp = compress(kv_cmp, w1, w2, pe)
    n_sel = T // SLC_BLOCK
    blocks = kv_slc.reshape(B, n_sel, SLC_BLOCK, 2, N_KV_HEADS, HEAD_DIM)
    bi = jnp.arange(B)[:, None, None, None]
    hi = jnp.arange(N_KV_HEADS)[None, :, None, None]
    fetch = lambda idx: blocks[bi, idx, :, :, hi, :]
    win_pad = jnp.pad(kv_win, ((0, 0), (WINDOW, 0), (0, 0), (0, 0), (0, 0)))

    def q_block(qs):
        qpos = qs + jnp.arange(Q_BLOCK)
        return nsa_core(lax.dynamic_slice_in_dim(q, qs, Q_BLOCK, 1), qpos,
                        lax.dynamic_slice_in_dim(gates, qs, Q_BLOCK, 1), cmp, fetch, n_sel,
                        lax.dynamic_slice_in_dim(win_pad, qs, WINDOW + Q_BLOCK, 1),
                        qs - WINDOW + jnp.arange(WINDOW + Q_BLOCK))

    out = lax.map(q_block, jnp.arange(T // Q_BLOCK, dtype=jnp.int32) * Q_BLOCK)
    return out.transpose(1, 0, 2, 3).reshape(B, T, MIX_ATTN)

def nsa_sample(q, kv_cmp, kv_slc, kv_win, gates, cache_cmp, cache_slc, cache_win, page_table, w1, w2, pe):
    DB, Tq = q.shape[:2]
    n_pages = page_table.shape[1]
    past_len = n_pages * PAGE_SIZE
    past_cmp = cache_cmp[page_table].reshape(DB, past_len, 2, N_KV_HEADS, HEAD_DIM)
    cmp = compress(jnp.concatenate([past_cmp, kv_cmp.astype(past_cmp.dtype)], 1), w1, w2, pe)

    nb_past = past_len // SLC_BLOCK
    nb_new = -(-Tq // SLC_BLOCK)
    n_sel = nb_past + nb_new
    bpp = PAGE_SIZE // SLC_BLOCK
    pool = cache_slc.reshape(-1, bpp, SLC_BLOCK, 2, N_KV_HEADS, HEAD_DIM)
    new_blocks = jnp.pad(kv_slc, ((0, 0), (0, nb_new * SLC_BLOCK - Tq), (0, 0), (0, 0), (0, 0)))
    new_blocks = new_blocks.reshape(DB, nb_new, SLC_BLOCK, 2, N_KV_HEADS, HEAD_DIM)
    bi = jnp.arange(DB)[:, None, None, None]
    hi = jnp.arange(N_KV_HEADS)[None, :, None, None]

    def fetch(idx):
        pj = jnp.minimum(idx, nb_past - 1)
        page = page_table[bi, pj // bpp]
        past = pool[page, pj % bpp, :, :, hi, :]
        new = new_blocks[bi, jnp.clip(idx - nb_past, 0, nb_new - 1), :, :, hi, :]
        return jnp.where((idx < nb_past)[..., None, None, None], past, new.astype(past.dtype))

    win_buf = cache_win.shape[1]
    win_all = jnp.concatenate([cache_win, kv_win.astype(cache_win.dtype)], 1)
    win_pos = past_len - win_buf + jnp.arange(win_buf + Tq)
    qpos = past_len + jnp.arange(Tq)
    out = nsa_core(q, qpos, gates, cmp, fetch, n_sel, win_all, win_pos)
    return out, win_all[:, -win_buf:]

def setup_inputs(seed: int = 0) -> dict:
    key = jax.random.key(seed)
    ks = jax.random.split(key, 32)
    nrm = lambda k, shape, scale: jax.random.normal(k, shape, F32) * scale
    n_pages = PAST_LEN // PAGE_SIZE
    used = DEC_BATCH * n_pages
    n_pool = used + max(1, used // 4)
    win_buf = min(WINDOW, PAST_LEN)
    page_table = jax.random.permutation(ks[0], n_pool)[:used].reshape(DEC_BATCH, n_pages).astype(jnp.int32)
    return {
        "x_prompt": nrm(ks[1], (BATCH, SEQ, D_MODEL), 1.0),
        "x_sample": nrm(ks[2], (DEC_BATCH, DEC_SEQ, D_MODEL), 1.0),
        "p_prompt": nrm(ks[3], (DEPTH, BATCH, SEQ, PLE_DIM), 1.0),
        "p_sample": nrm(ks[4], (DEPTH, DEC_BATCH, DEC_SEQ, PLE_DIM), 1.0),
        "cache_cmp_kv": nrm(ks[5], (DEPTH, n_pool, PAGE_SIZE, 2, N_KV_HEADS, HEAD_DIM), 1.0),
        "cache_slc_kv": nrm(ks[6], (DEPTH, n_pool, PAGE_SIZE, 2, N_KV_HEADS, HEAD_DIM), 1.0),
        "cache_win_kv": nrm(ks[7], (DEPTH, DEC_BATCH, win_buf, 2, N_KV_HEADS, HEAD_DIM), 1.0),
        "state_conv": nrm(ks[8], (DEPTH, DEC_BATCH, CONV_W - 1, CONV_CH), 0.5),
        "page_table": page_table,
        "g_attn": 1.0 + nrm(ks[9], (DEPTH, D_MODEL), 0.05),
        "w_in": nrm(ks[10], (DEPTH, D_MODEL, N_IN), D_MODEL ** -0.5),
        "w_cmp1": nrm(ks[11], (DEPTH, 2, CMP_BLOCK, HEAD_DIM, CMP_HID), (CMP_BLOCK * HEAD_DIM) ** -0.5),
        "w_cmp2": nrm(ks[12], (DEPTH, 2, CMP_HID, HEAD_DIM), CMP_HID ** -0.5),
        "pe_cmp": nrm(ks[13], (DEPTH, 2, CMP_BLOCK, HEAD_DIM), 0.1),
        "conv_w": nrm(ks[14], (DEPTH, CONV_W, CONV_CH), CONV_W ** -0.5),
        "conv_b": nrm(ks[15], (DEPTH, CONV_CH), 0.01),
        "ln_conv_g": 1.0 + nrm(ks[16], (DEPTH, CONV_CH), 0.05),
        "ln_conv_b": nrm(ks[17], (DEPTH, CONV_CH), 0.01),
        "w_out": nrm(ks[18], (DEPTH, D_MODEL, D_MODEL), D_MODEL ** -0.5),
        "g_mlp": 1.0 + nrm(ks[19], (DEPTH, D_MODEL), 0.05),
        "w_up": nrm(ks[20], (DEPTH, D_MODEL, D_FF), D_MODEL ** -0.5),
        "w_down": nrm(ks[21], (DEPTH, D_FF, D_MODEL), D_FF ** -0.5),
        "g_ple": 1.0 + nrm(ks[22], (DEPTH, D_MODEL), 0.05),
        "w_ple": nrm(ks[23], (DEPTH, PLE_DIM, D_MODEL), PLE_DIM ** -0.5),
        "w_ple_gate": nrm(ks[24], (DEPTH, D_MODEL, D_MODEL), D_MODEL ** -0.5),
        "g_final": 1.0 + nrm(ks[25], (D_MODEL,), 0.05),
    }

def reference(x_prompt, x_sample, p_prompt, p_sample, cache_cmp_kv, cache_slc_kv, cache_win_kv,
              state_conv, page_table, g_attn, w_in, w_cmp1, w_cmp2, pe_cmp, conv_w, conv_b,
              ln_conv_g, ln_conv_b, w_out, g_mlp, w_up, w_down, g_ple, w_ple, w_ple_gate, g_final):
    win_buf = cache_win_kv.shape[2]
    xp, xs = x_prompt, x_sample
    pc, psl, pw, pcv, sc, ssl, sw, scv = [], [], [], [], [], [], [], []
    for i in range(DEPTH):
        q, kc, ksl, kw, gt, u = mixer_inputs(xp, g_attn[i], w_in[i])
        attn = nsa_prompt(q, kc, ksl, kw, gt, w_cmp1[i], w_cmp2[i], pe_cmp[i])
        hist = jnp.pad(u, ((0, 0), (CONV_W - 1, 0), (0, 0)))
        conv = conv_tail(hist, conv_w[i], conv_b[i], ln_conv_g[i], ln_conv_b[i])
        xp = layer_tail(xp, jnp.concatenate([attn, conv], -1), w_out[i], g_mlp[i], w_up[i], w_down[i],
                        g_ple[i], w_ple[i], w_ple_gate[i], p_prompt[i])
        pc.append(kc)
        psl.append(ksl)
        pw.append(jnp.pad(kw, ((0, 0), (win_buf, 0), (0, 0), (0, 0), (0, 0)))[:, -win_buf:])
        pcv.append(hist[:, -(CONV_W - 1):])
        q, kc, ksl, kw, gt, u = mixer_inputs(xs, g_attn[i], w_in[i])
        attn, new_win = nsa_sample(q, kc, ksl, kw, gt, cache_cmp_kv[i], cache_slc_kv[i], cache_win_kv[i],
                                   page_table, w_cmp1[i], w_cmp2[i], pe_cmp[i])
        hist = jnp.concatenate([state_conv[i].astype(u.dtype), u], 1)
        conv = conv_tail(hist, conv_w[i], conv_b[i], ln_conv_g[i], ln_conv_b[i])
        xs = layer_tail(xs, jnp.concatenate([attn, conv], -1), w_out[i], g_mlp[i], w_up[i], w_down[i],
                        g_ple[i], w_ple[i], w_ple_gate[i], p_sample[i])
        sc.append(kc)
        ssl.append(ksl)
        sw.append(new_win)
        scv.append(hist[:, -(CONV_W - 1):])
    y_prompt = rmsnorm(xp, g_final)
    y_sample = rmsnorm(xs, g_final)
    return (y_prompt, y_sample, jnp.stack(pc), jnp.stack(psl), jnp.stack(pw), jnp.stack(pcv),
            jnp.stack(sc), jnp.stack(ssl), jnp.stack(sw), jnp.stack(scv))


_drawn_inputs = setup_inputs


def setup_inputs(seed=0):
    import zlib

    import numpy as np

    out = dict(_drawn_inputs(seed))
    spreads = {}
    factors = {'pe_cmp': 3.042, 'conv_b': 7.129, 'ln_conv_b': 8.0, 'g_ple': 22.639}
    for name, (base, spread) in spreads.items():
        noise = np.random.default_rng([zlib.crc32(name.encode()), seed]).standard_normal(out[name].shape)
        drawn = base * np.exp(spread * noise) if base else spread * noise
        out[name] = __import__('jax').numpy.asarray(drawn.astype(out[name].dtype))
    for name, factor in factors.items():
        out[name] = (out[name] * factor).astype(out[name].dtype)
    return out
```

```python
from contextlib import ExitStack

import concourse.bass as bass
from concourse import mybir

ALU = mybir.AluOpType
ACT = mybir.ActivationFunctionType
AX_X = mybir.AxisListType.X
F32 = mybir.dt.float32
F32R = mybir.dt.float32r
I32 = mybir.dt.int32
ds = bass.ds

P = 128
D = 1024
KT = D // P
T = 1024
QB = T // P
B, NEW = 8, 4
SR = B * NEW
R = T + SR
NCH = 3
CH = R // NCH
PAST, PAGE = 4096, 128
NPG = PAST // PAGE
N_POOL = 320
H, KVH, G, DH = 8, 2, 4, 64
PAIRS = H // KVH
KVC = 2 * KVH * DH
C, CW = 512, 31
CT = C // P
HIST = CW - 1
STRIDE, CBLK = 16, 32
NCS = PAST // STRIDE - 1
NCP = T // STRIDE - 1
SELB = 64
NSEL = PAST // SELB + 1
WIN = 512
FF = 4 * D
PLE = 256
EPS = 1e-6
NEG = -1e30
QSCALE = DH ** -0.5
COL_KV = H * DH
COL_GATE = COL_KV + 3 * KVC
COL_CONV = COL_GATE + 3 * H


def after(eng, sem, n):
    if isinstance(n, int) and n <= 0:
        return
    eng.wait_ge(sem, n)


def rounds(eng, n, steps):
    steps(0)
    if n > 1:
        with eng.Fori(1, n) as it:
            steps(it)


class Chip:

    def __init__(self, nc, ctx):
        self.nc, self.ctx = nc, ctx
        self.base = 16512
        self.sems = []

    def at(self, name, shape, dtype, offset):
        return self.nc.alloc_sbuf_tensor_at(name, shape, dtype, offset=self.base + offset)

    def sem(self, name):
        s = self.nc.alloc_semaphore(name=name)
        self.sems.append(s)
        return s

    def clear_semaphores(self, kept):
        self.nc.clear_and_free_semaphores([s for s in self.sems if s is not kept])
        self.nc.all_engine_barrier()
        self.sems = [kept]

    def store(self, eng, out, in_):
        eng.dma_start(out, in_).then_inc(self.stored, 16)
        self.n_stored += 16


K1 = 1024
XT_OFF = 0
RSTD_OFF = 33 * K1
KCS_OFF = RSTD_OFF + 4352
VCS_OFF = KCS_OFF + 8 * K1
SMALL_OFF = VCS_OFF + 8 * K1
AREA = 58 * K1


def build_program(nc, a):
    with ExitStack() as ctx:
        c = Chip(nc, ctx)
        c.a = a
        small = [SMALL_OFF]

        def keep(name, shape, dtype=F32):
            n = 4
            for s in shape[1:]:
                n *= s
            off = small[0]
            small[0] += -(-n // 32) * 32
            assert small[0] <= AREA
            return c.at(name, shape, dtype, off)

        c.ident = keep("ident", [P, P])
        c.ones = keep("ones", [P, P])
        c.pages = keep("pages", [1, B * NPG], I32)
        c.gains = keep("gains", [P, 4, KT])
        c.conv_w = keep("conv_w", [P, CT, CW])
        c.conv_v = keep("conv_v", [P, 3, CT])
        c.slope = keep("slope", [P, H])
        c.qscale = keep("qscale", [P, PAIRS])
        c.neg_slope = keep("neg_slope", [P, H])
        c.neg_row_slope = keep("neg_row_slope", [P, 1])
        c.row_slope = keep("row_slope", [P, 1])
        c.pe_bias = keep("pe_bias", [P, 2])
        c.gate_p = keep("gate_p", [P, QB, 3 * H])
        c.gate_s = keep("gate_s", [P, 2, 3])
        c.QB = keep("QB", [P, B, 32])
        c.eps = keep("eps", [P, 1])
        c.xT = c.at("xT", [P, KT, R], F32, XT_OFF)
        c.rstd = c.at("rstd", [P, R], F32, RSTD_OFF)
        c.KcS = c.at("KcS", [P, B, 256], F32, KCS_OFF)
        c.VcS = c.at("VcS", [P, 2, B, P], F32, VCS_OFF)
        constants(c)
        compress_sampled(c)
        load_x(c)
        project(c)
        regroup(c)
        conv_norm(c)
        compress_prompt(c)
        attend_prompt(c)
        attend_sampled(c)
        c.clear_semaphores(c.stored)
        out_projection(c)
        mlp(c)
        layer_embedding(c)
        finish(c)
        return c




def constants(c):
    nc, a = c.nc, c.a
    t_i = c.at("t_i", [P, 16], I32, AREA)
    t_j = c.at("t_j", [P, 16], I32, AREA + 64)
    t_rows = c.at("t_rows", [P, P], F32, AREA + 1024)
    t_conv = c.at("t_conv", [CW, C], F32, AREA + 2048)
    c.loaded = c.sem("small_loaded")
    c.stored = c.sem("outputs_stored")
    c.n_stored = 0
    made = c.sem("const_made")
    masked = c.sem("const_masked")
    with nc.psum_tensor("cps", [P, 512], F32) as cps, nc.Block() as block:
        trans = c.sem("const_transposed")

        @block.sync
        def _(sp):
            sp.dma_start(c.pages[0:1, :], a["page_table"].rearrange("(o b) n -> o (b n)", o=1)).then_inc(c.loaded, 16)
            for n, name in enumerate(("g_attn", "g_mlp", "g_ple")):
                sp.dma_start(t_rows[n * KT:(n + 1) * KT, :], a[name].rearrange("o (k p) -> (o k) p", p=P)).then_inc(c.loaded, 16)
            sp.dma_start(t_rows[3 * KT:4 * KT, :], a["g_final"].rearrange("(k p) -> k p", p=P)).then_inc(c.loaded, 16)
            for n, name in enumerate(("conv_b", "ln_conv_g", "ln_conv_b")):
                sp.dma_start(t_rows[32 + n * CT:32 + (n + 1) * CT, :], a[name].rearrange("o (k p) -> (o k) p", p=P)).then_inc(c.loaded, 16)

            sp.dma_start(t_conv[:, :], a["conv_w"].rearrange("o w f -> (o w) f")).then_inc(c.loaded, 16)
            for b in range(B):
                c.store(sp, a["sample_win"][0, b, 0:WIN - NEW], a["cache_win_kv"][0, b, NEW:WIN])
            c.store(sp, a["sample_conv"][0, :, 0:HIST - NEW, :], a["state_conv"][0, :, NEW:HIST, :])

        @block.gpsimd
        def _(pool):
            nc.gpsimd.memset(c.ident[:], 0.0).then_inc(made, 1)
            nc.gpsimd.memset(c.ones[:], 1.0).then_inc(made, 1)
            nc.gpsimd.memset(c.eps[:], EPS).then_inc(made, 1)
            pool.wait_ge(made, 3)
            nc.gpsimd.affine_select(out=c.ident[:], in_=c.ident[:], compare_op=ALU.not_equal, fill=1.0,
                                    base=0, pattern=[[-1, P]], channel_multiplier=1).then_inc(made, 1)
            nc.gpsimd.iota(t_i[:, 0:H], pattern=[[-1, H]], base=126, channel_multiplier=0).then_inc(made, 1)
            nc.gpsimd.iota(t_i[:, 8:9], pattern=[[0, 1]], base=0, channel_multiplier=1).then_inc(made, 1)
            pool.wait_ge(made, 6)
            nc.gpsimd.iota(t_i[0:DH, 12:16], pattern=[[1, PAIRS]], base=127 + 1 - 3, channel_multiplier=0).then_inc(made, 1)
            pool.wait_ge(made, 7)
            nc.gpsimd.iota(t_i[DH:P, 12:16], pattern=[[1, PAIRS]], base=127 + 5 - 3, channel_multiplier=0).then_inc(made, 1)

        @block.vector
        def _(dve):
            dve.wait_ge(made, 8)
            nc.vector.tensor_scalar(c.slope[:].bitcast(I32), t_i[:, 0:H], 23, None, ALU.logical_shift_left).then_inc(masked, 1)
            nc.vector.tensor_scalar(c.qscale[:].bitcast(I32), t_i[:, 12:16], 23, None, ALU.logical_shift_left).then_inc(masked, 1)
            nc.vector.tensor_scalar(t_j[:, 0:1], t_i[:, 8:9], 2, 7, ALU.logical_shift_right, ALU.bitwise_and).then_inc(masked, 1)
            dve.wait_ge(masked, 3)
            nc.vector.tensor_scalar(t_j[:, 1:2], t_j[:, 0:1], -1.0, 126.0, ALU.mult, ALU.add).then_inc(masked, 1)
            dve.wait_ge(masked, 4)
            nc.vector.tensor_scalar(c.row_slope[:].bitcast(I32), t_j[:, 1:2], 23, None, ALU.logical_shift_left).then_inc(masked, 1)
            dve.wait_ge(masked, 5)
            nc.vector.tensor_scalar(c.neg_slope[:], c.slope[:], -1.0, None, ALU.mult).then_inc(masked, 1)
            nc.vector.tensor_scalar(c.neg_row_slope[:], c.row_slope[:], -1.0, None, ALU.mult).then_inc(masked, 1)
            dve.wait_ge(trans, 1)
            nc.vector.tensor_copy(c.gains[:].rearrange("p a k -> p (a k)"), cps[:, 0:32]).then_inc(masked, 1)
            nc.vector.tensor_copy(c.conv_v[:].rearrange("p a k -> p (a k)"), cps[:, 32:44]).then_inc(masked, 1)
            nc.vector.tensor_copy(c.conv_w[:], cps[:, 64:64 + CT * 32].rearrange("p (k w) -> p k w", w=32)[:, :, 0:CW]).then_inc(masked, 1)

        @block.tensor
        def _(pe):
            pe.wait_ge(c.loaded, 9 * 16)
            pe.wait_ge(made, 4)
            for k in range(CT):
                nc.tensor.transpose(cps[:, 64 + 32 * k:64 + 32 * k + CW], t_conv[:, P * k:P * k + P], c.ident[0:CW, 0:CW])
            nc.tensor.transpose(cps[:, 0:44], t_rows[0:44, :], c.ident[0:44, 0:44]).then_inc(trans, 1)


def compress(c, name, n_units, tiles, pages_of, kc, vc, area, w_area, raw_w_area, weights=None):
    nc, a = c.nc, c.a
    quads = tiles // 4
    NC = 16 * tiles
    halves = -(-NC // P)
    off = [area]

    def sb(nm, shape, dtype=F32):
        n = 4
        for s in shape[1:]:
            n *= s
        o = off[0]
        off[0] += -(-n // 32) * 32
        return c.at(f"{name}_{nm}", shape, dtype, o)

    slots = min(2, n_units)
    raw = sb("raw", [P, quads, 4, 8 * DH])
    relaid = [sb(f"relaid{s}", [P, quads, 4, 8 * DH]) for s in range(slots)]
    Xhi = [sb(f"Xhi{s}", [P, 8, NC + 2], F32R if weights is None else F32) for s in range(2)]
    Xlo = [sb(f"Xlo{s}", [P, 8, NC + 2], F32R) for s in range(2)]
    hid = sb("hid", [P, 2, NC])
    if weights is None:
        w2 = sb("w2", [P, 2, DH])
        pe_rows = sb("pe_rows", [32, P])
        peT = sb("peT", [P, 32])
        off[0] = raw_w_area
        w1raw = sb("w1raw", [P, 32, P])
        off[0] = w_area
        w1hi = sb("w1hi", [P, 32, P], F32R)
        w1lo = sb("w1lo", [P, 32, P], F32R)
        passes = ((w1hi, Xhi), (w1hi, Xlo), (w1lo, Xhi))
    else:
        w1, w2 = weights
        passes = ((w1, Xhi),)

    w_loaded = c.sem(f"{name}_w_loaded")
    raw_loaded = [[c.sem(f"{name}_raw_loaded_{queue}{q}") for q in range(quads)] for queue in ("sp", "pool")]
    relaid_ready = c.sem(f"{name}_relaid_ready")
    w_split = c.sem(f"{name}_w_split")
    padded = c.sem(f"{name}_padded")
    turned = c.sem(f"{name}_turned")
    hi_ready = c.sem(f"{name}_hi_ready")
    lo_ready = c.sem(f"{name}_lo_ready") if weights is None else hi_ready
    mm_done = c.sem(f"{name}_layer1_done")
    gelu_done = c.sem(f"{name}_gelu_done")
    l2_done = c.sem(f"{name}_layer2_done")
    l2_kept = c.sem(f"{name}_layer2_kept")
    pe_ready = c.sem(f"{name}_pe_ready")
    w2_ready = c.sem(f"{name}_w2_loaded")
    CHS = 4
    per = 2 if n_units > 1 else 1
    n_rounds = n_units // per

    with (nc.psum_tensor(f"{name}_ps_x0", [P, 512], F32) as ps_x0, nc.psum_tensor(f"{name}_ps_x1", [P, 512], F32) as ps_x1,
          nc.psum_tensor(f"{name}_ps_h0", [P, 512], F32) as ps_h0, nc.psum_tensor(f"{name}_ps_h1", [P, 512], F32) as ps_h1,
          nc.psum_tensor(f"{name}_ps_o0", [P, 512], F32) as ps_o0, nc.psum_tensor(f"{name}_ps_o1", [P, 512], F32) as ps_o1,
          nc.psum_tensor(f"{name}_ps_pe", [P, 512], F32) as ps_pe,
          nc.Block() as block):
        ps_x, ps_h, ps_o = [ps_x0, ps_x1], [ps_h0, ps_h1], [ps_o0, ps_o1]

        def load(eng, engine_type, part):
            def steps(r):
                for s in range(per):
                    b = r * per + s
                    for q in range(quads):
                        pages = pages_of(engine_type, b, q, part)
                        after(eng, relaid_ready, (b - 1) * quads + q + 1)
                        for n, page in enumerate(pages):
                            half, i = n % 2, 2 * part + n // 2
                            eng.dma_start(raw[DH * half:DH * half + DH, q, i, :],
                                          page.rearrange("o q f -> (o q) f")).then_inc(raw_loaded[part][q], 16)
            rounds(eng, n_rounds, steps)

        @block.sync
        def _(sp):
            load(sp, mybir.EngineType.SP, 0)

        @block.gpsimd
        def _(pool):
            for s in range(2):
                nc.gpsimd.memset(Xhi[s][:, :, NC:NC + 2].bitcast(F32), 0.0).then_inc(padded, 1)
                nc.gpsimd.memset(Xlo[s][:, :, NC:NC + 2].bitcast(F32), 0.0).then_inc(padded, 1)
            load(pool, mybir.EngineType.Pool, 1)

        @block.scalar
        def _(act):
            if weights is None:
                act.dma_start(pe_rows[:, :], a["pe_cmp"].rearrange("o c (j e) d -> (o c j) (e d)", e=2)).then_inc(w_loaded, 16)
                for cc in range(2):
                    act.dma_start(w1raw[:, 16 * cc:16 * cc + 16, :],
                                  a["w_cmp1"][0, cc].rearrange("(j e) d n -> (e d) j n", e=2)).then_inc(w_loaded, 16)
                    act.dma_start(w2[:, cc, :], a["w_cmp2"][0, cc]).then_inc(w2_ready, 16)
                act.wait_ge(w_loaded, 48)
                nc.scalar.activation(w1hi[:], w1raw[:], ACT.Copy).then_inc(w_split, 1)

            def hi(b, u, ch, s):
                for q in range(quads):
                    v = u * quads + q
                    after(act, turned, v + 1)
                    after(act, mm_done, u - 1)
                    x = Xhi[ch % 2][:, :, 64 * q:64 * q + 64]
                    src = ps_x[(ch * quads + q) % 2][:].rearrange("p (n j) -> p j n", j=8)
                    nc.scalar.activation(x, src, ACT.Copy).then_inc(hi_ready, 1)

            def gelu(u, ch):
                after(act, mm_done, u + 1)
                after(act, l2_done, u - 1)
                nc.scalar.activation(hid[:, ch % 2, :], ps_h[ch % 2][:, 0:NC], ACT.Gelu_apprx_tanh,
                                     bias=c.pe_bias[:, ch // 2:ch // 2 + 1]).then_inc(gelu_done, 1)

            def steps(r):
                for s in range(per):
                    for ch in range(CHS):
                        u = (r * per + s) * CHS + ch
                        hi(r * per + s, u, ch, s)
                        if not (isinstance(u, int) and u == 0):
                            gelu(u - 1, (ch - 1) % CHS)
            if weights is None:
                act.wait_ge(pe_ready, 4)
            rounds(act, n_rounds, steps)
            gelu(n_units * CHS - 1, CHS - 1)

        @block.vector
        def _(dve):
            if weights is None:
                dve.wait_ge(w_split, 1)
                nc.vector.tensor_tensor(w1lo[:], w1raw[:], w1hi[:], ALU.subtract).then_inc(w_split, 1)
                dve.wait_ge(pe_ready, 1)
                nc.vector.tensor_copy(peT[:], ps_pe[:, 0:32]).then_inc(pe_ready, 1)
                dve.wait_ge(pe_ready, 3)
                nc.vector.tensor_copy(c.pe_bias[:], ps_pe[:, 32:34]).then_inc(pe_ready, 1)

            def lo(u, ch):
                for q in range(quads):
                    after(dve, hi_ready, u * quads + q + 1)
                    x = slice(64 * q, 64 * q + 64)
                    src = ps_x[(ch * quads + q) % 2][:].rearrange("p (n j) -> p j n", j=8)
                    nc.vector.tensor_tensor(Xlo[ch % 2][:, :, x], src, Xhi[ch % 2][:, :, x].bitcast(F32),
                                            ALU.subtract).then_inc(lo_ready, 1)

            def keep(b, u, ch):
                after(dve, l2_done, u + 1)
                h = ch % 2
                if ch < 2:
                    nc.vector.tensor_copy(kc(b, h), ps_o[ch % 2][DH * h:DH * h + DH, 0:NC]).then_inc(l2_kept, 1)
                else:
                    rows = min(P, NC)
                    nc.vector.tensor_copy(vc(b, h), ps_o[ch % 2][0:rows, 0:halves * DH].rearrange("p (f d) -> p f d", d=DH)).then_inc(l2_kept, 1)

            def relay(b, q, s):
                for part in range(2):
                    after(dve, raw_loaded[part][q], (b + 1) * 64)
                if q == 0:
                    after(dve, turned, (b - 1) * CHS * quads)
                for i in range(4):
                    cp = nc.vector.tensor_copy(relaid[s][:, q, i, :].rearrange("p (m e d) -> p m e d", e=2, d=DH),
                                               raw[:, q, i, :].rearrange("p (e m d) -> p m e d", e=2, d=DH))
                cp.then_inc(relaid_ready, 1)

            def steps(r, last=False):
                for s in range(per):
                    for ch in range(CHS):
                        u = (r * per + s) * CHS + ch
                        if weights is None:
                            lo(u, ch)
                        if ch < quads and not (last and s == per - 1):
                            relay(r * per + s + 1, ch, (s + 1) % slots)
                        if not (isinstance(u, int) and u < 2):
                            keep(r * per + s - (ch < 2), u - 2, (ch - 2) % CHS)
            for q in range(quads):
                relay(0, q, 0)
            steps(0, last=(n_rounds == 1))
            if n_rounds > 2:
                with dve.Fori(1, n_rounds - 1) as it:
                    steps(it)
            if n_rounds > 1:
                steps(n_rounds - 1, last=True)
            for ch in (2, 3):
                keep(n_units - 1, n_units * CHS - 4 + ch, ch)

        @block.tensor
        def _(pe):
            if weights is None:
                pe.wait_ge(w_loaded, 48)
                nc.tensor.transpose(ps_pe[:, 0:32], pe_rows[:, :], c.ident[0:32, 0:32]).then_inc(pe_ready, 1)
                pe.wait_ge(pe_ready, 2)
                for cc in range(2):
                    for j in range(16):
                        mm = nc.tensor.matmul(ps_pe[:, 32 + cc:33 + cc], w1raw[:, 16 * cc + j, :], peT[:, 16 * cc + j:16 * cc + j + 1],
                                              start=(j == 0), stop=(j == 15))
                mm.then_inc(pe_ready, 1)

            def turn(u, ch, s, b, part):
                for q in part:
                    v = u * quads + q
                    if ch == 0:
                        after(pe, relaid_ready, b * quads + q + 1)
                    after(pe, lo_ready, v - 1)
                    for i in range(4):
                        mm = nc.tensor.transpose(ps_x[(ch * quads + q) % 2][:, P * i:P * i + P],
                                                 relaid[s][:, q, i, P * ch:P * ch + P], c.ident[:])
                    mm.then_inc(turned, 1)

            def layer1(u, ch, part):
                if part == 0:
                    after(pe, lo_ready, (u + 1) * quads)
                    after(pe, gelu_done, u - 1)
                cc = ch // 2
                n = len(passes) * 8 * part
                for j in range(8 * part, 8 * part + 8):
                    xs = slice(j // 8, j // 8 + NC)
                    for w, x in passes:
                        mm = nc.tensor.matmul(ps_h[ch % 2][:, 0:NC], w[:, 16 * cc + j, :], x[ch % 2][:, j % 8, xs],
                                              start=(n == 0), stop=(n == 16 * len(passes) - 1))
                        n += 1
                if part == 1:
                    mm.then_inc(mm_done, 1)

            def layer2(u, ch):
                after(pe, gelu_done, u + 1)
                after(pe, l2_kept, u - 1)
                h = ch % 2
                if ch < 2:
                    mm = nc.tensor.matmul(ps_o[ch % 2][DH * h:DH * h + DH, 0:NC], w2[:, 0, :], hid[:, ch % 2, :], start=True, stop=True)
                else:
                    rows = min(P, NC)
                    for f in range(halves):
                        mm = nc.tensor.matmul(ps_o[ch % 2][0:rows, DH * f:DH * f + DH], hid[:, ch % 2, rows * f:rows * f + rows],
                                              w2[:, 1, :], start=True, stop=True)
                mm.then_inc(l2_done, 1)

            if weights is None:
                pe.wait_ge(w_split, 2)
                pe.wait_ge(w2_ready, 32)
            pe.wait_ge(padded, 4)

            def steps(r):
                for s in range(per):
                    for ch in range(CHS):
                        u = (r * per + s) * CHS + ch
                        for part in range(2):
                            turn(u, ch, s, r * per + s, range(part * quads // 2, (part + 1) * quads // 2))
                            if not (isinstance(u, int) and u < 1):
                                layer1(u - 1, (ch - 1) % CHS, part)
                        if not (isinstance(u, int) and u < 2):
                            layer2(u - 2, (ch - 2) % CHS)
            rounds(pe, n_rounds, steps)
            n = n_units * CHS
            layer1(n - 1, CHS - 1, 0)
            layer1(n - 1, CHS - 1, 1)
            layer2(n - 2, CHS - 2)
            layer2(n - 1, CHS - 1)


def compress_sampled(c):
    nc = c.nc
    pool_dram = c.a["cache_cmp_kv"].rearrange("o n (q e) c h d -> (o n) q (e c h d)", e=2)

    def pages_of(engine_type, b, q, part):
        _, pages = nc.values_load_multi_w_load_instructions(
            c.pages[0:1, ds(b * NPG + (8 * q + 4 * part), 4)], engines=[engine_type], min_val=0, max_val=N_POOL - 1)
        return [pool_dram[ds(page, 1)] for page in pages]

    compress(c, "cs", B, NPG // 2, pages_of,
             lambda b, h: c.KcS[DH * h:DH * h + DH, ds(b, 1), :].rearrange("p o n -> p (o n)"),
             lambda b, h: c.VcS[:, :, ds(b, 1), DH * h:DH * h + DH].rearrange("p f o d -> p f (o d)"),
             AREA, XT_OFF, AREA + 64 * K1)


PROJ_OFF = AREA
U_OFF = PROJ_OFF + 42240
US_OFF = U_OFF + 17376
A_OFF = AREA + 64000
W_OFF = A_OFF + 2 * 33792
LATE_OFF = AREA + 149504


def load_x(c):
    nc, a = c.nc, c.a
    rows = [c.at(f"x_rows{s}", [P, D], F32, PROJ_OFF + 4096 * s) for s in range(3)]
    st_rows = [c.at(f"state_rows{s}", [P, C], F32, PROJ_OFF + 12288 + 2048 * s) for s in range(2)]
    sq = [c.at(f"x_sq{s}", [P, R], F32, PROJ_OFF + 16384 + 4224 * s) for s in range(2)]
    c.u = c.at("u", [P, CT, HIST + R], F32, U_OFF)
    c.us = c.at("us", [P, CT, B, HIST + NEW], F32, US_OFF)
    c.Ahi = c.at("Ahi", [P, KT, R], F32R, A_OFF)
    c.Alo = c.at("Alo", [P, KT, R], F32R, A_OFF + 33792)
    c.x_spill = nc.dram_tensor("x_spill", [P, KT * R], F32, kind="Internal").ap()
    c.spilled = c.sem("x_spilled")
    loaded = [c.sem(f"x_rows_loaded{s}") for s in range(3)]
    st_loaded = c.sem("state_loaded")
    turned = c.sem("x_turned")
    kept_a, kept_v = c.sem("x_kept_by_act"), c.sem("x_kept_by_dve")
    st_kept, st_turned = c.sem("state_kept"), c.sem("state_turned")
    hi_ready, lo_ready, sq_ready, summed = c.sem("x_hi_ready"), c.sem("x_lo_ready"), c.sem("x_sq_ready"), c.sem("x_summed")
    norm = c.sem("x_norm")
    zeroed = c.sem("x_zeroed")
    NR = QB + 1
    with (nc.psum_tensor("ps_turn", [P, 4, 512], F32) as ps_turn, nc.psum_tensor("ps_sum", [P, NCH, 512], F32) as ps_sum,
          nc.psum_tensor("ps_state", [P, 512], F32) as ps_state, nc.Block() as block):
        def n_rows(r):
            return P if r < QB else SR

        @block.sync
        def _(sp):
            for s in range(2):
                sp.dma_start(st_rows[s][0:4 * HIST, :], a["state_conv"][0, 4 * s:4 * s + 4].rearrange("b t f -> (b t) f")).then_inc(st_loaded, 16)
            for r in range(NR):
                if r >= 3:
                    sp.wait_ge(turned, 2 * (r - 2))
                src = a["x_prompt"][0, P * r:P * r + P, :] if r < QB else a["x_sample"].rearrange("b t f -> (b t) f")
                sp.dma_start(rows[r % 3][0:n_rows(r), :], src).then_inc(loaded[r % 3], 16)
            sp.wait_ge(kept_a, NR)
            sp.wait_ge(kept_v, NR)
            sp.dma_start(c.x_spill, c.xT[:].rearrange("p k r -> p (k r)")).then_inc(c.spilled, 16)
            sp.wait_ge(c.spilled, 16)

        @block.gpsimd
        def _(pool):
            nc.gpsimd.memset(c.u[:, :, 0:HIST], 0.0).then_inc(zeroed, 1)

        @block.tensor
        def _(pe):
            for s in range(2):
                pe.wait_ge(st_loaded, 32)
                if s == 1:
                    pe.wait_ge(st_kept, 1)
                for k in range(CT):
                    mm = nc.tensor.transpose(ps_state[:, 120 * k:120 * k + 120], st_rows[s][0:120, P * k:P * k + P], c.ident[0:120, 0:120])
                mm.then_inc(st_turned, 1)
            for r in range(NR):
                pe.wait_ge(loaded[r % 3], 16 * (r // 3 + 1))
                n = n_rows(r)
                for half in range(2):
                    if r >= 2:
                        pe.wait_ge((kept_a, kept_v)[half], r - 1)
                    for k in range(4):
                        mm = nc.tensor.transpose(ps_turn[:, 2 * (r % 2) + half, n * k:n * k + n],
                                                 rows[r % 3][0:n, P * (4 * half + k):P * (4 * half + k) + P], c.ident[0:n, 0:n])
                    mm.then_inc(turned, 1)
            for k in range(KT):
                pe.wait_ge(sq_ready, k + 1)
                for j in range(NCH):
                    mm = nc.tensor.matmul(ps_sum[:, j, 0:CH], c.ones[:], sq[k % 2][:, CH * j:CH * j + CH],
                                          start=(k == 0), stop=(k == KT - 1))
                mm.then_inc(summed, 1)

        def keep(engine, r, half):
            n = n_rows(r)
            return engine(c.xT[:, 4 * half:4 * half + 4, P * r:P * r + n],
                          ps_turn[:, 2 * (r % 2) + half, 0:4 * n].rearrange("p (k n) -> p k n", n=n))

        @block.scalar
        def _(act):
            for r in range(NR):
                act.wait_ge(turned, 2 * r + 1)
                keep(lambda o, i: nc.scalar.activation(o, i, ACT.Copy), r, 0).then_inc(kept_a, 1)
            act.wait_ge(kept_a, NR)
            act.wait_ge(kept_v, NR)
            for k in range(KT):
                nc.scalar.activation(c.Ahi[:, k, :], c.xT[:, k, :], ACT.Copy, scale=c.gains[:, 0, k:k + 1]).then_inc(hi_ready, 1)
                if k >= 2:
                    act.wait_ge(summed, k - 1)
                nc.scalar.activation(sq[k % 2][:], c.xT[:, k, :], ACT.Square).then_inc(sq_ready, 1)
            act.wait_ge(norm, 1)
            nc.scalar.activation(c.rstd[:], c.rstd[:], ACT.Sqrt).then_inc(norm, 1)

        @block.vector
        def _(dve):
            for s in range(2):
                dve.wait_ge(st_turned, s + 1)
                nc.vector.tensor_copy(c.us[:, :, 4 * s:4 * s + 4, 0:HIST],
                                      ps_state[:, 0:480].rearrange("p (k b t) -> p k b t", k=CT, b=4)).then_inc(st_kept, 1)
            for r in range(NR):
                dve.wait_ge(turned, 2 * r + 2)
                keep(nc.vector.tensor_copy, r, 1).then_inc(kept_v, 1)
            dve.wait_ge(kept_v, NR)
            for k in range(KT):
                dve.wait_ge(hi_ready, k + 1)
                nc.vector.scalar_tensor_tensor(out=c.Alo[:, k, :], in0=c.xT[:, k, :], scalar=c.gains[:, 0, k:k + 1],
                                               in1=c.Ahi[:, k, :].bitcast(F32), op0=ALU.mult, op1=ALU.subtract).then_inc(lo_ready, 1)
            dve.wait_ge(summed, KT)
            nc.vector.tensor_scalar(c.rstd[:].rearrange("p (j n) -> p j n", n=CH), ps_sum[:, :, 0:CH], 1.0 / D, EPS,
                                    ALU.mult, ALU.add).then_inc(norm, 1)
            dve.wait_ge(norm, 2)
            nc.vector.reciprocal(c.rstd[:], c.rstd[:]).then_inc(norm, 1)


class Weights:

    def __init__(self, c, name, off, raw_slots=1, nk=KT, split_off=None):
        self.c, self.nk, self.raw_slots = c, nk, raw_slots
        self.raw = [c.at(f"{name}_raw{s}", [P, nk, P], F32, off + 512 * nk * s) for s in range(raw_slots)]
        o = off + 512 * nk * raw_slots if split_off is None else split_off
        self.hi = [c.at(f"{name}_hi{s}", [P, nk, P], F32R, o + 512 * nk * s) for s in range(2)]
        o += 1024 * nk
        self.lo = [c.at(f"{name}_lo{s}", [P, nk, P], F32R, o + 512 * nk * s) for s in range(2)]
        self.loaded = [c.sem(f"{name}_loaded{s}") for s in range(raw_slots)]
        self.hi_ready = c.sem(f"{name}_hi_ready")
        self.lo_ready = c.sem(f"{name}_lo_ready")
        self.done = c.sem(f"{name}_gemm_done")
        self.free = c.sem(f"{name}_psum_free")

    def load(self, sp, t, s, parts):
        rs = s % self.raw_slots
        after(sp, self.lo_ready, t - self.raw_slots + 1)
        for index, src in parts:
            sp.dma_start(self.raw[rs][index], src).then_inc(self.loaded[rs], 16)

    def split_hi(self, act, t, s, n_parts, nk=None):
        nk = nk or self.nk
        rs = s % self.raw_slots
        n = (t + 1) * 16 * n_parts if self.raw_slots == 1 else (t - s + 2) * 8 * n_parts
        after(act, self.loaded[rs], n)
        after(act, self.done, t - 1)
        self.c.nc.scalar.activation(self.hi[s][:, 0:nk, :], self.raw[rs][:, 0:nk, :], ACT.Copy).then_inc(self.hi_ready, 1)

    def split_lo(self, pool, t, s, nk=None):
        nk = nk or self.nk
        after(pool, self.hi_ready, t + 1)
        self.c.nc.gpsimd.tensor_tensor(self.lo[s][:, 0:nk, :], self.raw[s % self.raw_slots][:, 0:nk, :],
                                       self.hi[s][:, 0:nk, :].bitcast(F32), ALU.subtract).then_inc(self.lo_ready, 1)

    def multiply(self, pe, t, s, ps, xhi, xlo, nk=None, before=None):
        nk = nk or self.nk
        after(pe, self.lo_ready, t + 1)
        after(pe, self.free, t - 1)
        nc = self.c.nc
        for k in range(nk):
            if before is not None:
                before(k)
            for n, (w, x) in enumerate(((self.hi, xhi), (self.hi, xlo), (self.lo, xhi))):
                for j in range(NCH):
                    mm = nc.tensor.matmul(ps[:, j, 0:CH], w[s][:, k, :], x(k)[:, CH * j:CH * j + CH],
                                          start=(k == 0 and n == 0), stop=(k == nk - 1 and n == 2))
        mm.then_inc(self.done, 1)


def three(ap):
    return ap.rearrange("p (j n) -> p j n", n=CH)


def project(c):
    nc, a = c.nc, c.a
    c.proj = c.at("proj", [P, 10, R], F32, PROJ_OFF)
    c.y = c.at("y", [P, CT, R], F32, XT_OFF)
    c.gT = c.at("gT", [P, R], F32, XT_OFF + 17 * K1)
    W = Weights(c, "win", W_OFF)
    w_in = a["w_in"].rearrange("o (k p) n -> (o p) k n", p=P)
    act_done, dve_step, conv_step = c.sem("sigmoid_done"), c.sem("u_step"), c.sem("conv_step")
    g_step = c.sem("gate_step")
    EARLY = 15
    with nc.psum_tensor("ps_p0", [P, NCH, 512], F32) as ps0, nc.psum_tensor("ps_p1", [P, NCH, 512], F32) as ps1, nc.Block() as block:
        ps = [ps0, ps1]

        @block.sync
        def _(sp):
            def tile(t, s, col):
                W.load(sp, t, s, [((slice(0, P), slice(h, h + 4)), w_in[:, h:h + 4, ds(col, P)]) for h in (0, 4)])

            def conv(r):
                tile(2 * r, 0, r * P + COL_CONV + C)
                tile(2 * r + 1, 1, r * P + COL_CONV)
            rounds(sp, CT, conv)

            def queries(r):
                for s in range(2):
                    i = r * 2 + s
                    W.load(sp, i + 8, s, [((slice(0, P), slice(0, KT), slice(DH * e, DH * e + DH)), w_in[:, :, ds(i * DH + e * G * DH, DH)]) for e in range(2)])
            with sp.Fori(0, 2) as r:
                queries(r)

            def keys(r):
                for s in range(2):
                    tile(r * 2 + 12 + s, s, r * 2 * P + (COL_KV + s * P))
            with sp.Fori(0, 3) as r:
                keys(r)
            tile(18, 0, COL_GATE)

        @block.gpsimd
        def _(pool):
            def steps(r):
                for s in range(2):
                    W.split_lo(pool, r * 2 + s, s)
            rounds(pool, 9, steps)
            W.split_lo(pool, 18, 0)

        def uv(i):
            return c.u[:, ds(i, 1), HIST:HIST + R].rearrange("p o r -> p (o r)")

        @block.scalar
        def _(act):
            def conv(r):
                W.split_hi(act, r * 2, 0, 2)
                if not isinstance(r, int):
                    sig(r - 1)
                W.split_hi(act, r * 2 + 1, 1, 2)

            def sig(r):
                after(act, W.free, r * 2 + 1)
                nc.scalar.activation(uv(r), uv(r), ACT.Sigmoid).then_inc(act_done, 1)
            rounds(act, CT, conv)
            for s in range(2):
                W.split_hi(act, 2 * CT + s, s, 2)
                if s == 0:
                    sig(CT - 1)

            def rest(r):
                for s in range(2):
                    W.split_hi(act, r * 2 + s, s, 2)
            with act.Fori(5, 9) as r:
                rest(r)
            W.split_hi(act, 18, 0, 2)
            act.wait_ge(g_step, 1)
            nc.scalar.activation(c.gT[0:3 * H, :], c.gT[0:3 * H, :], ACT.Sigmoid).then_inc(g_step, 1)

        @block.tensor
        def _(pe):
            def steps(r):
                for s in range(2):
                    W.multiply(pe, r * 2 + s, s, ps[s], lambda k: c.Ahi[:, k, :], lambda k: c.Alo[:, k, :])
            rounds(pe, 9, steps)
            W.multiply(pe, 18, 0, ps[0], lambda k: c.Ahi[:, k, :], lambda k: c.Alo[:, k, :])

        @block.vector
        def _(dve):
            def gate(r):
                after(dve, W.done, r * 2 + 1)
                nc.vector.tensor_tensor(three(uv(r)), ps[0][:, :, 0:CH], three(c.rstd[:]), ALU.mult).then_inc(W.free, 1)

            def gated(r):
                after(dve, act_done, r + 1)
                after(dve, W.done, r * 2 + 2)
                nc.vector.tensor_tensor(three(uv(r)), ps[1][:, :, 0:CH], three(uv(r)), ALU.mult).then_inc(W.free, 1)
                after(dve, W.free, r * 2 + 2)
                nc.vector.tensor_tensor(uv(r), uv(r), c.rstd[:], ALU.mult).then_inc(dve_step, 1)
                after(dve, dve_step, r * 2 + 1)
                nc.vector.tensor_copy(c.us[:, ds(r, 1), :, HIST:HIST + NEW].rearrange("p o b t -> p (o b) t"),
                                      c.u[:, ds(r, 1), HIST + T:HIST + R].rearrange("p o (b t) -> p (o b) t", t=NEW)).then_inc(dve_step, 1)

            def flat(ap):
                return ap.rearrange("p o r -> p (o r)")

            def parts(k, tap):
                return ((flat(c.y[:, ds(k, 1), 0:T]), flat(c.u[:, ds(k, 1), ds(tap, T)])),
                        (flat(c.y[:, ds(k, 1), T:R]).rearrange("p (b t) -> p b t", t=NEW),
                         c.us[:, ds(k, 1), :, ds(tap, NEW)].rearrange("p o b t -> p (o b) t")))

            def first(k):
                for o, i in parts(k, 0):
                    st = nc.vector.tensor_scalar(o, i, flat(c.conv_w[:, ds(k, 1), 0:1]), c.conv_v[:, 0, ds(k, 1)], ALU.mult, ALU.add)
                st.then_inc(conv_step, 1)

            def tap_of(k, tap, before):
                after(dve, conv_step, before)
                for o, i in parts(k, tap):
                    st = nc.vector.scalar_tensor_tensor(out=o, in0=i, scalar=flat(c.conv_w[:, ds(k, 1), ds(tap, 1)]), in1=o,
                                                        op0=ALU.mult, op1=ALU.add)
                st.then_inc(conv_step, 1)

            gate(0)
            gated(0)

            def behind(r):
                gate(r)
                after(dve, dve_step, r * 2)
                first(r - 1)
                for tap in range(1, EARLY + 1):
                    tap_of(r - 1, tap, (r - 1) * (EARLY + 1) + tap)
                    if tap == EARLY // 2:
                        gated(r)
            with dve.Fori(1, CT) as r:
                behind(r)
            dve.wait_ge(dve_step, 2 * CT)
            first(CT - 1)
            base = (CT - 1) * (EARLY + 1) + 1
            late, whole = (CW - 1 - EARLY) // 5, (CW - 1) // 5
            order = [[(CT - 1, whole, j) for j in range(3)] + [(k, late, j) for j in range(2) for k in range(CT - 1)],
                     [(CT - 1, whole, j) for j in range(3, 6)] + [(k, late, 2) for k in range(CT - 1)]]
            flat_order = order[0] + order[1]
            per = len(flat_order)

            def tile(r):
                for s in range(2):
                    after(dve, W.done, r * 2 + 9 + s)
                    nc.vector.tensor_tensor(three(flat(c.proj[:, ds(r * 2 + s, 1), :])),
                                            ps[s][:, :, 0:CH], three(c.rstd[:]), ALU.mult).then_inc(W.free, 1)
                    for n, (k, each, j) in enumerate(order[s]):
                        at = n + s * len(order[0])
                        same = [m for m in range(per) if flat_order[m][0] == k]
                        if at != same[0]:
                            before = r * per + (base + max(m for m in same if m < at) + 1)
                        elif isinstance(r, int):
                            before = base if k == CT - 1 else (k + 1) * (EARLY + 1)
                        else:
                            before = (r - 1) * per + (base + same[-1] + 1)
                        tap_of(k, r * each + ((1 if k == CT - 1 else EARLY + 1) + j), before)
            rounds(dve, 5, tile)
            dve.wait_ge(W.done, 19)
            nc.vector.tensor_tensor(three(c.gT[0:3 * H, :]), ps[0][0:3 * H, :, 0:CH], three(c.rstd[0:3 * H, :]), ALU.mult).then_inc(g_step, 1)


def regroup(c):
    nc, a = c.nc, c.a
    c.KS = c.at("KS", [P, 2, KVH, T], F32R, AREA + 113408)
    c.V = c.at("V", [P, QB, 2, P], F32, AREA + 129792)
    c.Vn = c.at("Vn", [P, 2, P], F32, LATE_OFF)
    c.KnT = c.at("KnT", [P, 2, SR], F32, LATE_OFF + 1024)
    c.KcP = c.at("KcP", [P, 64], F32, LATE_OFF + 1280)
    c.VcP = c.at("VcP", [P, P], F32, LATE_OFF + 1536)
    Qhi = c.at("Qhi", [P, PAIRS, T], F32R, A_OFF)
    Qlo = c.at("Qlo", [P, PAIRS, T], F32R, A_OFF + 16384)
    Khi = c.at("Khi", [P, 2, T], F32R, A_OFF + 32768)
    Klo = c.at("Klo", [P, 2, T], F32R, A_OFF + 40960)
    rowbuf = [c.at(f"rowbuf{s}", [P, 3 * KVC], F32, AREA + 137984 + 3072 * s) for s in range(2)]
    crow = c.at("crow", [SR, 2, C], F32, AREA + 144128)
    c.q_dram = nc.dram_tensor("q_split", [PAIRS, KVH, 2, DH, T], F32, kind="Internal").ap()
    g_dram = nc.dram_tensor("gates_sampled", [3, 2, P], F32, kind="Internal").ap()
    turned, kept_a, kept_v = c.sem("kv_turned"), c.sem("kv_kept_by_act"), c.sem("kv_kept_by_dve")
    v_kept = c.sem("v_rows_kept")
    rows_stored = [c.sem(f"rows_stored{s}") for s in range(2)]
    hi_ready, lo_ready, moved = c.sem("qk_hi_ready"), c.sem("qk_lo_ready"), c.sem("qk_moved")
    small, small_kept = c.sem("small_turned"), c.sem("small_kept")
    g_moved = c.sem("gates_moved")
    qb_zero, qb_ready = c.sem("qb_zeroed"), c.sem("qb_ready")
    NR = QB + 1
    kv_out = [(a["prompt_cmp"][0, 0], a["sample_cmp"][0]), (a["prompt_slc"][0, 0], a["sample_slc"][0])]
    with (nc.psum_tensor("ps_kv0", [P, 2, 512], F32) as ps_kv0, nc.psum_tensor("ps_kv1", [P, 2, 512], F32) as ps_kv1,
          nc.psum_tensor("ps_c", [P, 2, 512], F32) as ps_c, nc.psum_tensor("ps_g", [P, 512], F32) as ps_g, nc.Block() as block):
        ps_kv = [ps_kv0, ps_kv1]

        def stored_rows(r):
            n = 0
            for q in range(r % 2, r + 1, 2):
                n += 16 * (3 if q >= QB // 2 else 2) if q < QB else 0
            return n

        @block.tensor
        def _(pe):
            for e, at in enumerate((HIST + T - SR, HIST + T)):
                for k in range(CT):
                    nc.tensor.transpose(ps_c[0:SR, e, P * k:P * k + P], c.u[:, k, at:at + SR], c.ident[:])
            for r in range(QB):
                mm = nc.tensor.transpose(ps_g[:, 24 * r:24 * r + 24], c.gT[0:24, P * r:P * r + P], c.ident[0:24, 0:24])
            mm.then_inc(small, 1)
            for r in range(NR):
                n = P if r < QB else SR
                if r >= 2:
                    pe.wait_ge(kept_a, r - 1)
                    pe.wait_ge(kept_v, r - 1)
                for t in range(6):
                    mm = nc.tensor.transpose(ps_kv[r % 2][0:n, t // 4, P * (t % 4):P * (t % 4) + P],
                                             c.proj[:, 4 + t, P * r:P * r + n], c.ident[:])
                mm.then_inc(turned, 1)

        @block.scalar
        def _(act):
            for i in range(PAIRS):
                nc.scalar.activation(Qhi[:, i, :], c.proj[:, i, 0:T], ACT.Copy, scale=c.qscale[:, i:i + 1]).then_inc(hi_ready, 1)
            for e in range(2):
                nc.scalar.activation(Khi[:, e, :], c.proj[:, 6 + 2 * e, 0:T], ACT.Copy).then_inc(hi_ready, 1)
            for r in range(NR):
                n = P if r < QB else SR
                act.wait_ge(turned, r + 1)
                if r >= 2:
                    act.wait_ge(v_kept, r - 1)
                    act.wait_ge(rows_stored[r % 2], stored_rows(r - 2))
                nc.scalar.activation(rowbuf[r % 2][0:n, 0:512], ps_kv[r % 2][0:n, 0, :], ACT.Copy).then_inc(kept_a, 1)
            for e in range(2):
                nc.scalar.activation(c.KnT[:, e, :], c.proj[:, 6 + 2 * e, T:R], ACT.Copy)
            act.wait_ge(qb_zero, 1)
            for e in range(KVH):
                for g in range(G):
                    h = G * e + g
                    q = nc.scalar.activation(c.QB[DH * e:DH * e + DH, :, NEW * h:NEW * h + NEW],
                                             c.proj[DH * e:DH * e + DH, g, T:R].rearrange("p (b t) -> p b t", t=NEW),
                                             ACT.Copy, scale=c.qscale[DH * e:DH * e + DH, g:g + 1])
            q.then_inc(qb_ready, 1)

        @block.vector
        def _(dve):
            dve.wait_ge(small, 1)
            nc.vector.tensor_copy(crow[:], ps_c[0:SR, :, :]).then_inc(small_kept, 1)
            nc.vector.tensor_copy(c.gate_p[:].rearrange("p q g -> p (q g)"), ps_g[:, 0:24 * QB]).then_inc(small_kept, 1)
            for i in range(PAIRS):
                dve.wait_ge(hi_ready, i + 1)
                nc.vector.scalar_tensor_tensor(out=Qlo[:, i, :], in0=c.proj[:, i, 0:T], scalar=c.qscale[:, i:i + 1],
                                               in1=Qhi[:, i, :].bitcast(F32), op0=ALU.mult, op1=ALU.subtract).then_inc(lo_ready, 1)
            for e in range(2):
                dve.wait_ge(hi_ready, PAIRS + e + 1)
                nc.vector.tensor_tensor(Klo[:, e, :], c.proj[:, 6 + 2 * e, 0:T], Khi[:, e, :].bitcast(F32), ALU.subtract).then_inc(lo_ready, 1)
            for r in range(NR):
                n = P if r < QB else SR
                dve.wait_ge(turned, r + 1)
                if r >= 2:
                    dve.wait_ge(v_kept, r - 1)
                    dve.wait_ge(rows_stored[r % 2], stored_rows(r - 2))
                nc.vector.tensor_copy(rowbuf[r % 2][0:n, 512:768], ps_kv[r % 2][0:n, 1, 0:256]).then_inc(kept_v, 1)

        @block.gpsimd
        def _(pool):
            nc.gpsimd.memset(c.QB[:], 0.0).then_inc(qb_zero, 1)
            nc.gpsimd.memset(c.Vn[:], 0.0).then_inc(qb_zero, 1)
            nc.gpsimd.memset(c.VcP[:], 0.0).then_inc(qb_zero, 1)
            pool.wait_ge(qb_zero, 3)
            for r in range(NR):
                n = P if r < QB else SR
                pool.wait_ge(kept_a, r + 1)
                pool.wait_ge(kept_v, r + 1)
                out = c.V[:, r, :, :] if r < QB else c.Vn[0:SR, :, :]
                nc.gpsimd.tensor_copy(out, rowbuf[r % 2][0:n, 256:768].rearrange("p (e f) -> p e f", e=2)[:, :, P:2 * P]).then_inc(v_kept, 1)

        @block.sync
        def _(sp):
            sp.wait_ge(small_kept, 2)
            c.store(sp, a["prompt_conv"][0, 0], crow[SR - HIST:SR, 0, :])
            c.store(sp, a["sample_conv"][0, :, HIST - NEW:HIST, :], crow[:, 1, :])
            for e in range(3):
                sp.dma_start(g_dram[e].rearrange("g (b h t) -> h (g b) t", h=H, t=NEW),
                             c.gT[H * e:H * e + H, T:R].rearrange("h (b t) -> h b t", t=NEW)).then_inc(g_moved, 16)
            sp.wait_ge(g_moved, 48)
            for e in range(3):
                sp.dma_start(c.gate_s[:, :, e], g_dram[e].rearrange("g p -> p g"), allow_slow_non_contiguous=True).then_inc(g_moved, 16)
            sp.wait_ge(lo_ready, PAIRS + 2)
            for n, part in enumerate((Qhi, Qlo)):
                for e in range(KVH):
                    sp.dma_start(c.q_dram[:, e, n].rearrange("i d r -> d i r"), part[DH * e:DH * e + DH, :, :].bitcast(F32)).then_inc(moved, 16)
            for n, part in enumerate((Khi, Klo)):
                for e in range(KVH):
                    sp.dma_start(c.KS[DH * n:DH * n + DH, :, e, :].bitcast(F32), part[DH * e:DH * e + DH, :, :].bitcast(F32)).then_inc(moved, 16)
            for r in range(NR):
                sp.wait_ge(kept_a, r + 1)
                sp.wait_ge(kept_v, r + 1)
                for e, (name_p, name_s) in enumerate((("prompt_cmp", "sample_cmp"), ("prompt_slc", "sample_slc"), ("prompt_win", "sample_win"))):
                    src = rowbuf[r % 2][:, KVC * e:KVC * e + KVC]
                    if r < QB:
                        r0 = P * r - (WIN if e == 2 else 0)
                        if r0 < 0:
                            continue
                        out = a[name_p][0, 0, r0:r0 + P].rearrange("t c h d -> t (c h d)")
                        sp.dma_start(out, src).then_inc(rows_stored[r % 2], 16)
                    elif e < 2:
                        c.store(sp, a[name_s][0].rearrange("b t c h d -> (b t) (c h d)"), src[0:SR, :])
                    else:
                        for b in range(B):
                            c.store(sp, a[name_s][0, b, WIN - NEW:WIN].rearrange("t c h d -> t (c h d)"), src[NEW * b:NEW * b + NEW, :])
            for s in range(2):
                sp.wait_ge(rows_stored[s], stored_rows(QB - 2 + s))
            sp.wait_ge(moved, 8 * 16)
            sp.wait_ge(g_moved, 6 * 16)
            sp.wait_ge(c.stored, c.n_stored)


def compress_prompt(c):
    nc = c.nc
    rows = c.a["prompt_cmp"].rearrange("o b (n q e) c h d -> (o b n) q (e c h d)", e=2, q=DH)
    compress(c, "cp", 1, 4, lambda engine_type, b, q, part: [rows[n:n + 1] for n in range(4 * part, 4 * part + 4)],
             lambda b, h: c.KcP[DH * h:DH * h + DH, :],
             lambda b, h: c.VcP[0:64, DH * h:DH * h + DH].rearrange("p (o d) -> p o d", o=1),
             AREA, None, None, weights=(c.w1, c.w2))


MIX_OFF = AREA + 69120
CLAMP = -1e20


def attend_prompt(c):
    nc = c.nc
    stage = [c.at(f"q_stage{s}", [P, KVH, 2, T], F32R, AREA + 16384 * s) for s in range(2)]
    S = [c.at(f"S{s}", [P, 1792], F32, AREA + 32768 + 7168 * s) for s in range(3)]
    PTs = [c.at(f"PT{s}", [P, 512], F32, AREA + 54272 + 2048 * s) for s in range(4)]
    far = c.at("far", [P, T + WIN + P + 120], F32, AREA + 62464)
    c.mixA = c.at("mixA", [P, PAIRS, R], F32, MIX_OFF + 512)
    KSc = c.at("KSc", [P, KVH, 64], F32R, LATE_OFF + 2048)
    Kc_hi = c.at("Kc_hi", [P, 64], F32R, LATE_OFF + 2560)
    Kc_lo = c.at("Kc_lo", [P, 64], F32R, LATE_OFF + 2816)
    mx = c.at("mx", [P, 3, 4], F32, LATE_OFF + 3072)
    nm = c.at("nm", [P, 3, 4], F32, LATE_OFF + 3136)
    sums = c.at("sums", [P, 3, 4], F32, LATE_OFF + 3200)
    wt = c.at("wt", [P, 3, 4], F32, LATE_OFF + 3264)
    Tslc, Twin, Tcmp = far[:, 0:T], far[:, T:T + WIN + P], far[:, T + WIN + P:]
    CMP = T + WIN + P

    UNITS = [(s, i, e) for s in range(2) for i in range(QB) for e in range(KVH)]
    NU = len(UNITS)
    groups = []
    for n, (s, i, e) in enumerate(UNITS):
        w0 = max(0, i - 4)
        blocks = [(0, k, P * k) for k in range(i + 1)] + [(1, k, T + P * (k - w0)) for k in range(w0, i + 1)] + [(2, 0, CMP)]
        for k in range(0, len(blocks), 4):
            groups.append((n, blocks[k:k + 4], k == 0, k + 4 >= len(blocks)))
    NG = len(groups)
    assert NG % 4 == 0
    unit_groups = [[k for k in range(NG) if groups[k][0] == n] for n in range(NU)]

    tables, table_done = c.sem("tables"), c.sem("table_done")
    kc_ready, kc_moved = c.sem("kc_split"), c.sem("kc_moved")
    q_loaded = [c.sem(f"q_loaded{s}") for s in range(2)]
    qk_done, s_read, nm_ready, exp_done = c.sem("qk_done"), c.sem("s_read"), c.sem("nm_ready"), c.sem("exp_done")
    wt_step, wt_ready = c.sem("wt_step"), c.sem("wt_ready")
    slc_scaled, win_scaled = c.sem("slc_scaled"), c.sem("win_scaled")
    t_done, pv_done = c.sem("p_turned"), c.sem("pv_done")
    kept = [c.sem("pt_kept_by_act"), c.sem("pt_kept_by_dve")]
    o_kept = c.sem("o_kept")

    def kept_count(r, k):
        return r * (NG // 2) + k // 2 + 1

    with (nc.psum_tensor("ps_S", [P, 2, 512], F32) as ps_S, nc.psum_tensor("ps_W", [P, 2, 512], F32) as ps_W,
          nc.psum_tensor("ps_T0", [P, 512], F32) as ps_T0, nc.psum_tensor("ps_T1", [P, 512], F32) as ps_T1,
          nc.psum_tensor("ps_O0", [P, 512], F32) as ps_O0, nc.psum_tensor("ps_O1", [P, 512], F32) as ps_O1,
          nc.Block() as block):
        ps_T, ps_O = [ps_T0, ps_T1], [ps_O0, ps_O1]

        @block.sync
        def _(sp):
            sp.wait_ge(kc_ready, 2)
            for n, part in enumerate((Kc_hi, Kc_lo)):
                for e in range(KVH):
                    sp.dma_start(KSc[DH * n:DH * n + DH, e, :].bitcast(F32), part[DH * e:DH * e + DH, :].bitcast(F32)).then_inc(kc_moved, 16)

            def steps(r):
                for s in range(2):
                    for half in range(2):
                        src = c.q_dram[ds(r * 2 + s, 1)].rearrange("o e n d t -> (o d) e n t")
                        if half == 0:
                            after(sp, qk_done, (r - 1) * NU + NU // 2 * (s + 1))
                        sp.dma_start(stage[s][DH * half:DH * half + DH, :, :, :].bitcast(F32), src).then_inc(q_loaded[s], 16)
            rounds(sp, 2, steps)

        @block.gpsimd
        def _(pool):
            nc.gpsimd.iota(Tslc, pattern=[[1, T]], base=P - T, channel_multiplier=-1, allow_small_or_imprecise_dtypes=True).then_inc(tables, 1)
            nc.gpsimd.iota(Twin, pattern=[[1, WIN + P]], base=-WIN, channel_multiplier=-1, allow_small_or_imprecise_dtypes=True).then_inc(tables, 1)
            nc.gpsimd.iota(Tcmp, pattern=[[STRIDE, 120]], base=CBLK - 1 - 56 * STRIDE, channel_multiplier=-1, allow_small_or_imprecise_dtypes=True).then_inc(tables, 1)
            for s in range(3):
                nc.gpsimd.memset(S[s][:, CMP:CMP + P], 0.0).then_inc(tables, 1)
            pool.wait_ge(tables, 6)
            nc.gpsimd.affine_select(out=Tslc, in_=Tslc, compare_op=ALU.is_ge, fill=NEG, base=T - P, pattern=[[-1, T]], channel_multiplier=1).then_inc(tables, 1)
            nc.gpsimd.affine_select(out=Twin, in_=Twin, compare_op=ALU.is_ge, fill=NEG, base=WIN, pattern=[[-1, WIN + P]], channel_multiplier=1).then_inc(tables, 1)
            nc.gpsimd.affine_select(out=Tcmp, in_=Tcmp, compare_op=ALU.is_ge, fill=NEG, base=56 * STRIDE - CBLK + 1, pattern=[[-STRIDE, 120]], channel_multiplier=1).then_inc(tables, 1)
            pool.wait_ge(tables, 9)
            nc.gpsimd.affine_select(out=Twin, in_=Twin, compare_op=ALU.is_gt, fill=NEG, base=0, pattern=[[1, WIN + P]], channel_multiplier=-1).then_inc(table_done, 1)

            def steps(r):
                for n, (s, i, e) in enumerate(UNITS):
                    w = P * (min(i, 4) + 1)
                    sl = S[n % 3]
                    after(pool, wt_ready, r * NU + n + 1)
                    nc.gpsimd.tensor_tensor(sl[:, T:T + w], sl[:, T:T + w], wt[:, n % 3, 2:3].to_broadcast([P, w]), ALU.mult)
                    nc.gpsimd.tensor_tensor(sl[:, CMP:CMP + 64], sl[:, CMP:CMP + 64], wt[:, n % 3, 0:1].to_broadcast([P, 64]), ALU.mult).then_inc(win_scaled, 1)
            rounds(pool, 2, steps)

        @block.tensor
        def _(pe):
            def qk(r, n):
                s, i, e = UNITS[n]
                if i == 0 and e == 0:
                    after(pe, q_loaded[s], (r + 1) * 32)
                after(pe, s_read, r * NU + n)
                w0 = max(0, i - 4)
                nw = P * (i + 1 - w0)
                parts = [(ps_S[:, 0, 0:min(512, P * (i + 1))], c.KS[:, 0, e, 0:min(512, P * (i + 1))])]
                if i >= 4:
                    parts.append((ps_S[:, 1, 0:P * (i - 3)], c.KS[:, 0, e, 512:P * (i + 1)]))
                parts.append((ps_W[:, 0, 0:min(512, nw)], c.KS[:, 1, e, P * w0:P * w0 + min(512, nw)]))
                if nw > 512:
                    parts.append((ps_W[:, 1, 0:P], c.KS[:, 1, e, P * w0 + 512:P * w0 + nw]))
                parts.append((ps_W[:, 1, P:P + 64], KSc[:, e, :]))
                for out, keys in parts:
                    for hl in range(2):
                        mm = nc.tensor.matmul(out, stage[s][:, e, hl, P * i:P * i + P], keys, start=(hl == 0), stop=(hl == 1))
                mm.then_inc(qk_done, 1)

            def turn(r, k):
                n, blocks, first, _ = groups[k]
                if first:
                    after(pe, slc_scaled, r * NU + n + 1)
                if blocks[-1][0] and (first or not groups[k - 1][1][-1][0]):
                    after(pe, win_scaled, r * NU + n + 1)
                after(pe, kept[k % 2], kept_count(r, k - 2))
                for j, (_, _, col) in enumerate(blocks):
                    mm = nc.tensor.transpose(ps_T[k % 2][:, P * j:P * j + P], S[n % 3][:, col:col + P], c.ident[:])
                mm.then_inc(t_done, 1)

            def pv(r, k):
                n, blocks, first, last = groups[k]
                s, i, e = UNITS[n]
                after(pe, kept[k % 2], kept_count(r, k))
                if first and e == 0:
                    after(pe, o_kept, r * (NU // 2) + n // 2 - 1)
                for j, (br, kb, _) in enumerate(blocks):
                    v = c.VcP[:, DH * e:DH * e + DH] if br == 2 else c.V[:, kb, br, DH * e:DH * e + DH]
                    mm = nc.tensor.matmul(ps_O[i % 2][DH * e:DH * e + DH, 0:P], v, PTs[k % 4][:, P * j:P * j + P],
                                          start=(first and j == 0), stop=(last and j == len(blocks) - 1))
                if last:
                    mm.then_inc(pv_done, 1)

            def steps(r):
                qk(r, 0)
                qk(r, 1)
                for n in range(NU):
                    if n + 2 < NU:
                        qk(r, n + 2)
                    for k in unit_groups[n]:
                        turn(r, k)
                        if k >= 2:
                            pv(r, k - 2)
                pv(r, NG - 2)
                pv(r, NG - 1)
            pe.wait_ge(kc_moved, 64)
            rounds(pe, 2, steps)

        @block.scalar
        def _(act):
            nc.scalar.activation(Kc_hi[:], c.KcP[:], ACT.Copy).then_inc(kc_ready, 1)

            def exps(r, n, part=range(3)):
                s, i, e = UNITS[n]
                h = r * 2 + (s + G * e)
                w = P * (min(i, 4) + 1)
                sl, z = S[n % 3], n % 3
                slope = c.slope[:, ds(h, 1)]
                if 0 in part:
                    after(act, nm_ready, r * NU + n + 1)
                for br, a0, width in [((1, 0, P * (i + 1)), (2, T, w), (0, CMP, 64))[p] for p in part]:
                    x = nc.scalar.activation(sl[:, a0:a0 + width], sl[:, a0:a0 + width], ACT.Exp, bias=nm[:, z, br:br + 1],
                                             scale=slope, accum_out=sums[:, z, br:br + 1])
                if 2 in part:
                    x.then_inc(exp_done, 1)

            def keep(r, k):
                after(act, t_done, r * NG + k + 1)
                w = P * len(groups[k][1])
                nc.scalar.activation(PTs[k % 4][:, 0:w], ps_T[0][:, 0:w], ACT.Copy).then_inc(kept[0], 1)

            def keep_o(r, m):
                s, i = m // QB, m % QB
                after(act, pv_done, r * NU + 2 * m + 2)
                nc.scalar.activation(c.mixA[:, ds(r * 2 + s, 1), P * i:P * i + P].rearrange("p o n -> p (o n)"),
                                     ps_O[i % 2][:, 0:P], ACT.Copy).then_inc(o_kept, 1)

            def steps(r):
                exps(r, 0)
                exps(r, 1)
                for n in range(NU):
                    even = [k for k in unit_groups[n] if k % 2 == 0]
                    for k in even[:1]:
                        keep(r, k)
                    if n + 2 < NU:
                        exps(r, n + 2, (0,))
                    for k in even[1:]:
                        keep(r, k)
                    if n + 2 < NU:
                        exps(r, n + 2, (1, 2))
                    if n >= 2 and n % 2 == 0:
                        keep_o(r, n // 2 - 1)
                keep_o(r, NU // 2 - 1)
            rounds(act, 2, steps)

        @block.vector
        def _(dve):
            dve.wait_ge(kc_ready, 1)
            nc.vector.tensor_tensor(Kc_lo[:], c.KcP[:], Kc_hi[:].bitcast(F32), ALU.subtract).then_inc(kc_ready, 1)
            dve.wait_ge(table_done, 1)

            def scores(r, n):
                s, i, e = UNITS[n]
                h = r * 2 + (s + G * e)
                w = P * (min(i, 4) + 1)
                nk = P * (i + 1)
                sl, z = S[n % 3], n % 3
                after(dve, qk_done, r * NU + n + 1)
                both = ps_S[:].rearrange("p a b -> p (a b)")
                wins = ps_W[:].rearrange("p a b -> p (a b)")
                for br, a0, width, src, tab in (
                        (1, 0, nk, both[:, 0:nk], Tslc[:, T - nk:T]), (2, T, w, wins[:, 0:w], Twin[:, WIN + P - w:WIN + P]),
                        (0, CMP, 64, wins[:, 512 + P:512 + P + 64], Tcmp[:, 56 - 8 * i:120 - 8 * i])):
                    x = nc.vector.tensor_tensor_reduce(sl[:, a0:a0 + width], src, tab, 1.0, -3e38, ALU.add, ALU.max, mx[:, z, br:br + 1])
                x.then_inc(s_read, 1)
                after(dve, s_read, r * NU + n + 1)
                nc.vector.tensor_scalar(nm[:, z, 0:3], mx[:, z, 0:3], CLAMP, c.neg_slope[:, ds(h, 1)], ALU.max, ALU.mult).then_inc(nm_ready, 1)

            def weigh(r, n):
                s, i, e = UNITS[n]
                h = r * 2 + (s + G * e)
                sl, z = S[n % 3], n % 3
                after(dve, exp_done, r * NU + n + 1)
                nc.vector.tensor_scalar(sums[:, z, 0:3], sums[:, z, 0:3], 1e-30, None, ALU.max).then_inc(wt_step, 1)
                after(dve, wt_step, (r * NU + n) * 2 + 1)
                nc.vector.reciprocal(sums[:, z, 0:3], sums[:, z, 0:3]).then_inc(wt_step, 1)
                after(dve, wt_step, (r * NU + n) * 2 + 2)
                gate = c.gate_p[:, i, :].rearrange("p (b h) -> p b h", h=H)[:, :, ds(h, 1)].rearrange("p b o -> p (b o)")
                nc.vector.tensor_tensor(wt[:, z, 0:3], sums[:, z, 0:3], gate, ALU.mult).then_inc(wt_ready, 1)
                after(dve, wt_ready, r * NU + n + 1)
                nc.vector.tensor_scalar(sl[:, 0:P * (i + 1)], sl[:, 0:P * (i + 1)], wt[:, z, 1:2], None, ALU.mult).then_inc(slc_scaled, 1)

            def keep(r, k):
                after(dve, t_done, r * NG + k + 1)
                w = P * len(groups[k][1])
                nc.vector.tensor_copy(PTs[k % 4][:, 0:w], ps_T[1][:, 0:w]).then_inc(kept[1], 1)

            def steps(r):
                scores(r, 0)
                scores(r, 1)
                weigh(r, 0)
                for n in range(NU):
                    if n + 2 < NU:
                        scores(r, n + 2)
                    odd = [k for k in unit_groups[n] if k % 2 == 1]
                    for k in odd[:1]:
                        keep(r, k)
                    if n + 1 < NU:
                        weigh(r, n + 1)
                    for k in odd[1:]:
                        keep(r, k)
            rounds(dve, 2, steps)


def attend_sampled(c):
    nc, a = c.nc, c.a
    GRP, ROWS = 4, 32
    NQ = NPG // 4
    QK_ = 4 * P
    off = [AREA]

    def sb(name, shape, dtype=F32):
        n = 4
        for s in shape[1:]:
            n *= s
        o = off[0]
        off[0] += -(-n // 32) * 32
        return c.at("s_" + name, shape, dtype, o)

    Dist = sb("dist", [P, PAST])
    Masked = sb("masked", [P, PAST])
    S = sb("S", [P, PAST + P])
    Sw = sb("Sw", [P, WIN + P])
    Pc = sb("Pc", [P, 256])
    Pst = [sb(f"Pst{s}", [P, QK_]) for s in range(2)]
    PT = [sb(f"PT{s}", [P, 4, P]) for s in range(2)]
    Osb = sb("Osb", [P, P])
    Gm = sb("Gm", [P, P])
    Dcmp = sb("Dcmp", [P, 256])
    Dw = sb("Dw", [P, WIN])
    Dn = sb("Dn", [P, 2, SR])
    pi = sb("pi", [P, 8], I32)
    pf = sb("pf", [P, 8])
    mxs = sb("mxs", [P, 3, 16])
    m3 = sb("m3", [P, 4])
    nm = sb("nm", [P, 4])
    sums = sb("sums", [P, 4])
    wt = sb("wt", [P, 4])
    bonus = sb("bonus", [P, 72])
    score = sb("score", [P, 72])
    left1 = sb("left1", [P, 72])
    left2 = sb("left2", [P, 72])
    top = sb("top", [P, 16])
    selb = sb("selb", [P, 72])
    imp = sb("imp", [P, 64])
    assert off[0] <= MIX_OFF + 512
    off[0] = MIX_OFF + 512 + 4 * PAIRS * R
    Kraw = [sb(f"Kraw{s}", [P, 16, P]) for s in range(2)]
    KT_ = [sb(f"KT{s}", [P, GRP, QK_]) for s in range(2)]
    Vraw = [sb(f"Vraw{s}", [P, 16, P]) for s in range(2)]
    assert off[0] <= LATE_OFF
    t_seq, t_tok = S[:, 0:SR], S[:, 64:64 + SR]
    t_g1, t_g2, t_m = S[:, 128:256], S[:, 256:384], S[:, 512:1024]

    iotas, cols, tabs = c.sem("s_iotas"), c.sem("s_cols"), c.sem("s_tabs")
    k_loaded = [[c.sem(f"s_k{s}_by_sp"), c.sem(f"s_k{s}_by_pool")] for s in range(2)]
    v_loaded = [[c.sem(f"s_v{s}_by_sp"), c.sem(f"s_v{s}_by_pool")] for s in range(2)]
    k_turned, s_done, s_read = c.sem("s_k_turned"), c.sem("s_scores_done"), c.sem("s_scores_read")
    kt_kept = [c.sem("s_kt_kept_by_act"), c.sem("s_kt_kept_by_dve")]
    first_done, first_read = c.sem("s_first_scores"), c.sem("s_first_read")
    step, masked = c.sem("s_dve_step"), c.sem("s_masked")
    imp_done, exp_done = c.sem("s_imp_done"), c.sem("s_exp_done")
    pst_ready, p_turned, pt_kept, pv_done = c.sem("s_pst_ready"), c.sem("s_p_turned"), c.sem("s_pt_kept"), c.sem("s_pv_done")
    head_ready, q_added = c.sem("s_head_ready"), c.sem("s_quad_added")
    o_sb, o_turned, o_kept = c.sem("s_o_sb"), c.sem("s_o_turned"), c.sem("s_o_kept")
    NQ1 = NQ + 1
    slc = a["cache_slc_kv"].rearrange("o n t c h d -> (o n) t c (h d)")
    win = a["cache_win_kv"].rearrange("o b (j t) c h d -> (o b) j t c (h d)", t=P)

    def quads(eng, body):
        body(0, 0)
        body(1, 1)
        with eng.Fori(1, NQ // 2) as r:
            body(r * 2, 0)
            body(r * 2 + 1, 1)
        body(NQ, 0)

    def used(gr, q):
        n = q + NQ1 * gr
        return n if isinstance(q, int) and q == 0 else n - 1

    def arrived(gr, q, s):
        if isinstance(q, int):
            return 128 * ((5 if s == 0 else 4) * gr + q // 2 + 1)
        return (q - s) * 64 + 128 * ((5 if s == 0 else 4) * gr + 1)

    def load(eng, engine_type, members, gr, q, s, part, ring, sem, use_sem, per):
        for bb in members:
            b = GRP * gr + bb
            window = isinstance(q, int) and q == NQ
            if not window:
                _, pages = nc.values_load_multi_w_load_instructions(
                    c.pages[0:1, ds(q * 4 + b * NPG, 4)], engines=[engine_type], min_val=0, max_val=N_POOL - 1)
            if bb == members[0]:
                after(eng, use_sem, used(gr, q) * per)
            for j in range(4):
                src = win[b, j, :, part, :] if window else slc[ds(pages[j], 1), :, part, :].rearrange("o t f -> (o t) f")
                eng.dma_start(ring[s][:, 4 * bb + j, :], src).then_inc(sem[s][members[0] // 2], 16)

    def loads(eng, engine_type, members):
        for gr in range(2):
            quads(eng, lambda q, s: load(eng, engine_type, members, gr, q, s, 0, Kraw, k_loaded, k_turned, GRP))
            quads(eng, lambda q, s: load(eng, engine_type, members, gr, q, s, 1, Vraw, v_loaded, pv_done, 1))

    with (nc.psum_tensor("ps_KT0", [P, 512], F32) as ps_KT0, nc.psum_tensor("ps_KT1", [P, 512], F32) as ps_KT1,
          nc.psum_tensor("ps_s0", [P, 512], F32) as ps_s0, nc.psum_tensor("ps_s1", [P, 512], F32) as ps_s1,
          nc.psum_tensor("ps_P0", [P, 512], F32) as ps_P0, nc.psum_tensor("ps_P1", [P, 512], F32) as ps_P1,
          nc.psum_tensor("ps_o", [P, 512], F32) as ps_o, nc.psum_tensor("ps_first", [P, 512], F32) as ps_f,
          nc.Block() as block):
        ps_KT, ps_s, ps_P = [ps_KT0, ps_KT1], [ps_s0, ps_s1], [ps_P0, ps_P1]
        FS, FW, FI = 256, 256 + SR, 256 + 2 * SR

        @block.sync
        def _(sp):
            loads(sp, mybir.EngineType.SP, (0, 1))

        @block.gpsimd
        def _(pool):
            f = dict(allow_small_or_imprecise_dtypes=True, channel_multiplier=0)
            nc.gpsimd.iota(pi[:, 0:1], pattern=[[0, 1]], base=0, channel_multiplier=1).then_inc(iotas, 1)
            nc.gpsimd.iota(Dist[:], pattern=[[1, PAST]], base=-PAST, **f).then_inc(iotas, 1)
            nc.gpsimd.iota(Dcmp[:], pattern=[[STRIDE, 256]], base=CBLK - 1 - PAST, **f).then_inc(iotas, 1)
            nc.gpsimd.iota(Dw[:], pattern=[[1, WIN]], base=-WIN, **f).then_inc(iotas, 1)
            nc.gpsimd.iota(t_seq, pattern=[[1, B], [0, NEW]], base=0, **f).then_inc(iotas, 1)
            nc.gpsimd.iota(t_tok, pattern=[[0, B], [1, NEW]], base=0, **f).then_inc(iotas, 1)
            nc.gpsimd.iota(t_g1, pattern=[[1, 8], [0, 16]], base=0, **f).then_inc(iotas, 1)
            nc.gpsimd.iota(t_g2, pattern=[[0, 32], [1, 4]], base=0, **f).then_inc(iotas, 1)
            nc.gpsimd.memset(bonus[:], 0.0).then_inc(iotas, 1)
            nc.gpsimd.memset(Sw[:, WIN:WIN + P], 0.0).then_inc(iotas, 1)
            nc.gpsimd.memset(score[:, 64:65], 1e4).then_inc(iotas, 1)
            pool.wait_ge(iotas, 11)
            nc.gpsimd.memset(bonus[:, 0:1], 1e4).then_inc(iotas, 1)
            nc.gpsimd.memset(bonus[:, 63:64], 1e4).then_inc(iotas, 1)
            nc.gpsimd.memset(S[:, PAST:PAST + P], 0.0).then_inc(iotas, 1)
            pool.wait_ge(iotas, 14)
            loads(pool, mybir.EngineType.Pool, (2, 3))

        @block.tensor
        def _(pe):
            for gr in range(2):
                if gr:
                    pe.wait_ge(first_read, gr)
                    pe.wait_ge(imp_done, 2 * gr)
                for bb in range(GRP):
                    b = GRP * gr + bb
                    rows = slice(ROWS * bb, ROWS * bb + ROWS)
                    nc.tensor.matmul(ps_f[rows, 0:256], c.QB[:, b, :], c.KcS[:, b, :], start=True, stop=True)
                    nc.tensor.matmul(ps_f[rows, FS:FS + SR], c.QB[:, b, :], c.KnT[:, 0, :], start=True, stop=True)
                    mm = nc.tensor.matmul(ps_f[rows, FW:FW + SR], c.QB[:, b, :], c.KnT[:, 1, :], start=True, stop=True)
                mm.then_inc(first_done, 1)
                pe.wait_ge(step, STEPS * gr + IMP)
                nc.tensor.matmul(ps_f[:, FI:FI + 64], Gm[:], imp[:], start=True, stop=True).then_inc(imp_done, 1)

                def turn(q, s):
                    n = q + NQ1 * gr
                    for queue in range(2):
                        after(pe, k_loaded[s][queue], arrived(gr, q, s))
                    for bb in range(GRP):
                        after(pe, kt_kept[bb % 2], n * 2 + (bb // 2 - 0))
                        for j in range(4):
                            mm = nc.tensor.transpose(ps_KT[bb % 2][:, P * j:P * j + P], Kraw[s][:, 4 * bb + j, :], c.ident[:])
                        mm.then_inc(k_turned, 1)

                def scores(q, s):
                    n = q + NQ1 * gr
                    for e in range(2):
                        after(pe, kt_kept[e], n * 2 + 2)
                    after(pe, s_read, used(gr, q))
                    for bb in range(GRP):
                        mm = nc.tensor.matmul(ps_s[s][ROWS * bb:ROWS * bb + ROWS, :], c.QB[:, GRP * gr + bb, :], KT_[s][:, bb, :], start=True, stop=True)
                    mm.then_inc(s_done, 1)

                def quad(q, s):
                    turn(q, s)
                    if not (isinstance(q, int) and q == 0):
                        scores(q - 1, 1 - s)
                quads(pe, quad)
                scores(NQ, 0)

                def pv(q, s, vs, last=False):
                    for j in range(4):
                        for bb in range(GRP):
                            mm = nc.tensor.matmul(ps_o[ROWS * bb:ROWS * bb + ROWS, 0:P], PT[s][:, j, ROWS * bb:ROWS * bb + ROWS], vs(j, bb),
                                                  start=(q is None and j == 0), stop=(last and j == 3))
                    return mm
                t0 = (NQ1 + 1) * gr
                pe.wait_ge(head_ready, gr + 1)
                if gr:
                    pe.wait_ge(pt_kept, t0)
                    pe.wait_ge(o_sb, gr)
                for j, src in enumerate((S[:, PAST:PAST + P], Sw[:, WIN:WIN + P], Pc[:, 0:P], Pc[:, P:2 * P])):
                    mm = nc.tensor.transpose(ps_P[1][:, P * j:P * j + P], src, c.ident[:])
                mm.then_inc(p_turned, 1)

                def pv_head():
                    pe.wait_ge(pt_kept, t0 + 1)
                    pv(None, 1, lambda j, bb: c.Vn[:, j, :] if j < 2 else c.VcS[:, j - 2, GRP * gr + bb, :])

                def pv_quad(q, s, last=False):
                    after(pe, pt_kept, q + (t0 + 2))
                    for queue in range(2):
                        after(pe, v_loaded[s][queue], arrived(gr, q, s))
                    pv(q, s, lambda j, bb: Vraw[s][:, 4 * bb + j, :], last).then_inc(pv_done, 1)

                def turn_p(q, s):
                    n = q + NQ1 * gr
                    after(pe, pst_ready, n + 1)
                    after(pe, pt_kept, q + (t0 if not (isinstance(q, int) and q == 0) else t0))
                    for j in range(4):
                        mm = nc.tensor.transpose(ps_P[s][:, P * j:P * j + P], Pst[s][:, P * j:P * j + P], c.ident[:])
                    mm.then_inc(p_turned, 1)

                def quad_v(q, s):
                    turn_p(q, s)
                    if isinstance(q, int) and q == 0:
                        pv_head()
                    else:
                        pv_quad(q - 1, 1 - s)
                quads(pe, quad_v)
                pv_quad(NQ, 0, last=True)
                pe.wait_ge(o_sb, gr + 1)
                nc.tensor.transpose(ps_KT[0][:, 0:P], Osb[:], c.ident[:]).then_inc(o_turned, 1)
                pe.wait_ge(o_kept, gr + 1)

        @block.scalar
        def _(act):
            for gr in range(2):
                act.wait_ge(step, STEPS * gr + NMC)
                nc.scalar.activation(Pc[:], Pc[:], ACT.Exp, bias=nm[:, 0:1], scale=c.row_slope[:, 0:1], accum_out=sums[:, 0:1]).then_inc(exp_done, 1)

                def keep(q, s):
                    n = q + NQ1 * gr
                    for bb in (0, 2):
                        after(act, k_turned, n * GRP + (bb + 1))
                        if bb == 0:
                            after(act, s_done, used(gr, q))
                        nc.scalar.activation(KT_[s][:, bb, :], ps_KT[0][:, :], ACT.Copy).then_inc(kt_kept[0], 1)
                quads(act, keep)
                act.wait_ge(step, STEPS * gr + NMS)
                nc.scalar.activation(S[:, 0:PAST + SR], S[:, 0:PAST + SR], ACT.Exp, bias=nm[:, 1:2], scale=c.row_slope[:, 0:1], accum_out=sums[:, 1:2]).then_inc(exp_done, 1)
                nc.scalar.activation(Sw[:, 0:WIN + SR], Sw[:, 0:WIN + SR], ACT.Exp, bias=nm[:, 2:3], scale=c.row_slope[:, 0:1], accum_out=sums[:, 2:3]).then_inc(exp_done, 1)
                act.wait_ge(step, STEPS * gr + WTS)

                def weigh(q, s):
                    n = q + NQ1 * gr
                    after(act, p_turned, used(gr, q) + (gr + 1 if gr or not (isinstance(q, int) and q < 2) else 0))
                    if isinstance(q, int) and q == NQ:
                        w = nc.scalar.activation(Pst[s][:], Sw[:, 0:WIN], ACT.Copy, scale=wt[:, 2:3])
                    else:
                        w = nc.scalar.activation(Pst[s][:], S[:, ds(q * QK_, QK_)], ACT.Copy, scale=wt[:, 1:2])
                    w.then_inc(pst_ready, 1)
                quads(act, weigh)
                act.wait_ge(pv_done, NQ1 * (gr + 1))
                nc.scalar.activation(Osb[:], ps_o[:, 0:P], ACT.Copy).then_inc(o_sb, 1)

        @block.vector
        def _(dve):
            n_cols = [0]

            def col(ins):
                n_cols[0] += 1
                ins.then_inc(cols, 1)
                dve.wait_ge(cols, n_cols[0])
            dve.wait_ge(iotas, 14)
            V_ = nc.vector
            col(V_.tensor_scalar(pi[:, 1:2], pi[:, 0:1], 3, None, ALU.bitwise_and))
            col(V_.tensor_scalar(pi[:, 2:3], pi[:, 0:1], 4, None, ALU.logical_shift_right))
            col(V_.tensor_scalar(pi[:, 3:4], pi[:, 0:1], 5, None, ALU.logical_shift_right))
            col(V_.tensor_copy(pf[:, 1:4], pi[:, 1:4]))
            tok, key, seq = pf[:, 1:2], pf[:, 2:3], pf[:, 3:4]
            col(V_.tensor_scalar(Dist[:], Dist[:], tok, None, ALU.subtract))
            col(V_.tensor_scalar(Dcmp[:], Dcmp[:], tok, None, ALU.subtract))
            col(V_.tensor_scalar(Dw[:], Dw[:], tok, None, ALU.subtract))
            col(V_.tensor_scalar(t_m[:, 0:256], Dcmp[:], 0.0, NEG, ALU.is_gt, ALU.mult))
            col(V_.tensor_tensor(Dcmp[:], Dcmp[:], t_m[:, 0:256], ALU.add))
            col(V_.tensor_scalar(t_m, Dw[:], -float(WIN), NEG, ALU.is_le, ALU.mult))
            col(V_.tensor_tensor(Dw[:], Dw[:], t_m, ALU.add))
            col(V_.tensor_scalar(t_tok, t_tok, tok, None, ALU.subtract))
            for gr in range(2):
                col(V_.tensor_scalar(t_m[:, 0:SR], t_seq, seq, float(GRP * gr), ALU.subtract, ALU.not_equal))
                col(V_.tensor_scalar(t_m[:, 64:64 + SR], t_tok, 0.0, None, ALU.is_gt))
                col(V_.tensor_tensor(t_m[:, 0:SR], t_m[:, 0:SR], t_m[:, 64:64 + SR], ALU.max))
                col(V_.scalar_tensor_tensor(out=Dn[:, gr, :], in0=t_m[:, 0:SR], scalar=NEG, in1=t_tok, op0=ALU.mult, op1=ALU.add))
            col(V_.tensor_scalar(t_m[:, 0:P], t_g1, key, None, ALU.is_equal))
            col(V_.scalar_tensor_tensor(out=Gm[:], in0=t_g2, scalar=tok, in1=t_m[:, 0:P], op0=ALU.is_equal, op1=ALU.mult))

            n_step = [0]

            def link(ins, name=None):
                n_step[0] += 1
                assert name is None or name == (n_step[0] - 1) % STEPS + 1, (name, n_step[0])
                ins.then_inc(step, 1)
                dve.wait_ge(step, n_step[0])

            for gr in range(2):
                dve.wait_ge(first_done, gr + 1)
                if gr:
                    dve.wait_ge(p_turned, NQ1 + 1)
                V_.tensor_tensor_reduce(S[:, PAST:PAST + SR], ps_f[:, FS:FS + SR], Dn[:, gr, :], 1.0, -3e38, ALU.add, ALU.max, mxs[:, 1, 9:10])
                V_.tensor_tensor_reduce(Sw[:, WIN:WIN + SR], ps_f[:, FW:FW + SR], Dn[:, gr, :], 1.0, -3e38, ALU.add, ALU.max, mxs[:, 2, 1:2])
                V_.tensor_tensor_reduce(Pc[:], ps_f[:, 0:256], Dcmp[:], 1.0, -3e38, ALU.add, ALU.max, m3[:, 0:1]).then_inc(first_read, 1)
                dve.wait_ge(first_read, gr + 1)
                link(V_.tensor_scalar(nm[:, 0:1], m3[:, 0:1], CLAMP, c.neg_row_slope[:, 0:1], ALU.max, ALU.mult), NMC)
                dve.wait_ge(exp_done, 3 * gr + 1)
                link(V_.tensor_scalar(sums[:, 0:1], sums[:, 0:1], 1e-30, None, ALU.max))
                link(V_.reciprocal(sums[:, 0:1], sums[:, 0:1]))
                link(V_.tensor_scalar(Pc[:], Pc[:], sums[:, 0:1], None, ALU.mult))
                link(V_.tensor_reduce(imp[:], Pc[:].rearrange("p (j x) -> p j x", x=4), AX_X, ALU.add))
                link(V_.tensor_tensor(imp[:, 1:64], imp[:, 1:64], Pc[:, 3:252:4], ALU.add), IMP)
                dve.wait_ge(imp_done, 2 * gr + 1)
                V_.tensor_tensor(score[:, 0:64], ps_f[:, FI:FI + 64], bonus[:, 0:64], ALU.add).then_inc(imp_done, 1)
                dve.wait_ge(imp_done, 2 * gr + 2)
                link(V_.max(top[:, 0:8], score[:, 0:NSEL]))
                link(V_.match_replace(left1[:, 0:NSEL], top[:, 0:8], score[:, 0:NSEL], NEG))
                link(V_.max(top[:, 8:16], left1[:, 0:NSEL]))
                link(V_.match_replace(left2[:, 0:NSEL], top[:, 8:16], left1[:, 0:NSEL], NEG))
                link(V_.tensor_scalar(selb[:, 0:NSEL], left2[:, 0:NSEL], -1e29, NEG, ALU.is_gt, ALU.mult), SEL)
                V_.tensor_tensor(Masked[:].rearrange("p (j k) -> p j k", k=SELB), Dist[:].rearrange("p (j k) -> p j k", k=SELB),
                                 selb[:, 0:64].rearrange("p (j o) -> p j o", o=1).to_broadcast([P, 64, SELB]), ALU.add).then_inc(masked, 1)
                dve.wait_ge(masked, gr + 1)

                def keep(q, s):
                    n = q + NQ1 * gr
                    for bb in (1, 3):
                        after(dve, k_turned, n * GRP + (bb + 1))
                        if bb == 1:
                            after(dve, s_done, used(gr, q))
                        V_.tensor_copy(KT_[s][:, bb, :], ps_KT[1][:, :]).then_inc(kt_kept[1], 1)

                def read(q, s):
                    after(dve, s_done, q + (NQ1 * gr + 1))
                    if isinstance(q, int) and q == NQ:
                        x = V_.tensor_tensor_reduce(Sw[:, 0:WIN], ps_s[s][:, :], Dw[:], 1.0, -3e38, ALU.add, ALU.max, mxs[:, 2, 0:1])
                    else:
                        V_.tensor_tensor(S[:, ds(q * QK_, QK_)], ps_s[s][:, :], Masked[:, ds(q * QK_, QK_)], ALU.add).then_inc(q_added, 1)
                        after(dve, q_added, q + (NQ * gr + 1))
                        x = V_.tensor_reduce(mxs[:, 1, ds(q, 1)], S[:, ds(q * QK_, QK_)], AX_X, ALU.max)
                    x.then_inc(s_read, 1)

                def quad(q, s):
                    keep(q, s)
                    if not (isinstance(q, int) and q == 0):
                        read(q - 1, 1 - s)
                quads(dve, quad)
                read(NQ, 0)
                dve.wait_ge(s_read, NQ1 * (gr + 1))
                link(V_.tensor_tensor(mxs[:, 1, 8:9], mxs[:, 1, 9:10], mxs[:, 1, 9:10], ALU.max))
                link(V_.tensor_reduce(m3[:, 1:2], mxs[:, 1, 0:10], AX_X, ALU.max))
                link(V_.tensor_reduce(m3[:, 2:3], mxs[:, 2, 0:2], AX_X, ALU.max))
                link(V_.tensor_scalar(nm[:, 1:3], m3[:, 1:3], CLAMP, c.neg_row_slope[:, 0:1], ALU.max, ALU.mult), NMS)
                dve.wait_ge(exp_done, 3 * gr + 3)
                link(V_.tensor_scalar(sums[:, 1:3], sums[:, 1:3], 1e-30, None, ALU.max))
                link(V_.reciprocal(sums[:, 1:3], sums[:, 1:3]))
                link(V_.tensor_tensor(wt[:, 1:3], sums[:, 1:3], c.gate_s[:, gr, 1:3], ALU.mult), WTS)
                link(V_.tensor_scalar(S[:, PAST:PAST + SR], S[:, PAST:PAST + SR], wt[:, 1:2], None, ALU.mult))
                link(V_.tensor_scalar(Sw[:, WIN:WIN + SR], Sw[:, WIN:WIN + SR], wt[:, 2:3], None, ALU.mult))
                V_.tensor_scalar(Pc[:], Pc[:], c.gate_s[:, gr, 0:1], None, ALU.mult).then_inc(head_ready, 1)

                def keep_p(n, s):
                    after(dve, p_turned, n + ((NQ1 + 1) * gr + 1))
                    V_.tensor_copy(PT[s][:].rearrange("p j r -> p (j r)"), ps_P[s][:, :]).then_inc(pt_kept, 1)
                keep_p(0, 1)

                def keep_q(q, s):
                    if isinstance(q, int) and q == 0:
                        after(dve, pv_done, NQ1 * gr)
                    elif not (isinstance(q, int) and q == 1):
                        after(dve, pv_done, q + (NQ1 * gr - 1))
                    keep_p(q + 1, s)
                quads(dve, keep_q)
                dve.wait_ge(o_turned, gr + 1)
                for e in range(KVH):
                    out = c.mixA[DH * e:DH * e + DH, :, T + SR // 2 * gr:T + SR // 2 * (gr + 1)].rearrange("p g (b t) -> p g b t", t=NEW)
                    for bb in range(GRP):
                        src = ps_KT[0][DH * e:DH * e + DH, ROWS * bb + 16 * e:ROWS * bb + 16 * e + 16].rearrange("p (g t) -> p g t", t=NEW)
                        o = V_.tensor_copy(out[:, :, bb, :], src)
                o.then_inc(o_kept, 1)


NMC, IMP, SEL, NMS, WTS, STEPS = 1, 6, 11, 15, 18, 20


HID_OFF = AREA
ACT_OFF = AREA + 67584
RAW_OFF = AREA + 135168
SQ_OFF = RAW_OFF + 8192


def conv_norm(c):
    nc, a = c.nc, c.a
    temps = AREA + 42240
    mean = c.at("ln_mean", [P, R], F32, temps)
    rs = c.at("ln_rs", [P, R], F32, temps + 4224)
    sq = [c.at(f"ln_sq{s}", [P, R], F32, temps + 8448 + 4224 * s) for s in range(2)]
    c.w1 = c.at("w1_prompt", [P, 32, P], F32, AREA + 96768)
    c.w2 = c.at("w2_prompt", [P, 2, DH], F32, AREA + 96768 - 512)
    summed, centred, sq_ready, sq_used = c.sem("ln_summed"), c.sem("ln_centred"), c.sem("ln_sq_ready"), c.sem("ln_sq_used")
    stat, scaled, swished, loaded = c.sem("ln_stat"), c.sem("ln_scaled"), c.sem("ln_swished"), c.sem("w12_loaded")
    with nc.psum_tensor("ps_l0", [P, NCH, 512], F32) as ps0, nc.psum_tensor("ps_l1", [P, NCH, 512], F32) as ps1, nc.Block() as block:

        @block.sync
        def _(sp):
            for cc in range(2):
                sp.dma_start(c.w1[:, 16 * cc:16 * cc + 16, :], a["w_cmp1"][0, cc].rearrange("(j e) d n -> (e d) j n", e=2)).then_inc(loaded, 16)
                sp.dma_start(c.w2[:, cc, :], a["w_cmp2"][0, cc]).then_inc(loaded, 16)
            sp.dma_start(c.xT[:, CT:KT, :].rearrange("p k r -> p (k r)"), c.x_spill[:, CT * R:KT * R]).then_inc(loaded, 16)
            sp.wait_ge(loaded, 80)

        @block.tensor
        def _(pe):
            for k in range(CT):
                for j in range(NCH):
                    mm = nc.tensor.matmul(ps0[:, j, 0:CH], c.ones[:], c.y[:, k, CH * j:CH * j + CH], start=(k == 0), stop=(k == CT - 1))
            mm.then_inc(summed, 1)
            for k in range(CT):
                pe.wait_ge(sq_ready, k + 1)
                for j in range(NCH):
                    mm = nc.tensor.matmul(ps1[:, j, 0:CH], c.ones[:], sq[k % 2][:, CH * j:CH * j + CH], start=(k == 0), stop=(k == CT - 1))
                mm.then_inc(sq_used, 1)

        @block.scalar
        def _(act):
            for k in range(CT):
                act.wait_ge(centred, k + 1)
                if k >= 2:
                    act.wait_ge(sq_used, k - 1)
                nc.scalar.activation(sq[k % 2][:], c.y[:, k, :], ACT.Square).then_inc(sq_ready, 1)
            act.wait_ge(stat, 2)
            nc.scalar.activation(rs[:], rs[:], ACT.Sqrt).then_inc(stat, 1)
            for k in range(CT):
                act.wait_ge(scaled, k + 1)
                nc.scalar.activation(c.y[:, k, :], c.y[:, k, :], ACT.Silu, bias=c.conv_v[:, 2, k:k + 1]).then_inc(swished, 1)

        @block.vector
        def _(dve):
            dve.wait_ge(summed, 1)
            nc.vector.tensor_scalar(three(mean[:]), ps0[:, :, 0:CH], 1.0 / C, None, ALU.mult).then_inc(stat, 1)
            dve.wait_ge(stat, 1)
            for k in range(CT):
                nc.vector.tensor_tensor(c.y[:, k, :], c.y[:, k, :], mean[:], ALU.subtract).then_inc(centred, 1)
            dve.wait_ge(sq_used, CT)
            nc.vector.tensor_scalar(three(rs[:]), ps1[:, :, 0:CH], 1.0 / C, EPS, ALU.mult, ALU.add).then_inc(stat, 1)
            dve.wait_ge(stat, 3)
            nc.vector.reciprocal(rs[:], rs[:]).then_inc(stat, 1)
            dve.wait_ge(stat, 4)
            for k in range(CT):
                nc.vector.scalar_tensor_tensor(out=c.y[:, k, :], in0=c.y[:, k, :], scalar=c.conv_v[:, 1, k:k + 1], in1=rs[:],
                                               op0=ALU.mult, op1=ALU.mult).then_inc(scaled, 1)


class NextNorm:

    def __init__(self, c, name, gain, x_ready, before=0, split=True):
        self.c, self.gain, self.split = c, gain, split
        self.x_ready, self.before = x_ready, before
        self.hi = c.sem(f"{name}_next_hi")
        self.lo = c.sem(f"{name}_next_lo")
        self.sq_ready = c.sem(f"{name}_sq_ready")
        self.added = c.sem(f"{name}_sq_added")

    def act(self, act, j, s):
        c, nc = self.c, self.c.nc
        after(act, self.added, j - 1)
        after(act, self.x_ready, j + (self.before + 1))
        if not isinstance(j, int):
            act.wait_ge(self.x_ready, self.before + 1)
        x = c.xT[:, ds(j, 1), :].rearrange("p o r -> p (o r)")
        if self.split:
            nc.scalar.activation(c.Ahi2[:, ds(j, 1), :].rearrange("p o r -> p (o r)"), x, ACT.Copy,
                                 scale=c.gains[:, self.gain, ds(j, 1)]).then_inc(self.hi, 1)
        nc.scalar.activation(c.sq[s][:], x, ACT.Square).then_inc(self.sq_ready, 1)

    def dve(self, dve, j, s):
        c, nc = self.c, self.c.nc
        if self.split:
            after(dve, self.hi, j + 1)
            nc.vector.scalar_tensor_tensor(out=c.Alo2[:, ds(j, 1), :].rearrange("p o r -> p (o r)"), in0=c.xT[:, ds(j, 1), :].rearrange("p o r -> p (o r)"),
                                           scalar=c.gains[:, self.gain, ds(j, 1)],
                                           in1=c.Ahi2[:, ds(j, 1), :].rearrange("p o r -> p (o r)").bitcast(F32), op0=ALU.mult, op1=ALU.subtract).then_inc(self.lo, 1)

    def pool(self, pool, j, s):
        c, nc = self.c, self.c.nc
        after(pool, self.sq_ready, j + 1)
        if isinstance(j, int) and j == 0:
            nc.gpsimd.tensor_tensor(c.ssq[:], c.sq[0][:], c.zeros[:].to_broadcast([P, R]), ALU.add).then_inc(self.added, 1)
        else:
            after(pool, self.added, j)
            nc.gpsimd.tensor_tensor(c.ssq[:], c.ssq[:], c.sq[s][:], ALU.add).then_inc(self.added, 1)


def inverse_rms(c, name, out):
    nc = c.nc
    summed, stat = c.sem(f"{name}_summed"), c.sem(f"{name}_stat")
    with nc.psum_tensor(f"{name}_ps", [P, NCH, 512], F32) as ps, nc.Block() as block:
        @block.tensor
        def _(pe):
            for j in range(NCH):
                mm = nc.tensor.matmul(ps[:, j, 0:CH], c.ones[:], c.ssq[:, CH * j:CH * j + CH], start=True, stop=True)
            mm.then_inc(summed, 1)

        @block.vector
        def _(dve):
            dve.wait_ge(summed, 1)
            nc.vector.tensor_scalar(three(out[:]), ps[:, :, 0:CH], 1.0 / D, EPS, ALU.mult, ALU.add).then_inc(stat, 1)
            dve.wait_ge(stat, 2)
            nc.vector.reciprocal(out[:], out[:]).then_inc(stat, 1)

        @block.scalar
        def _(act):
            act.wait_ge(stat, 1)
            nc.scalar.activation(out[:], out[:], ACT.Sqrt).then_inc(stat, 1)


def out_projection(c):
    nc, a = c.nc, c.a
    c.Mhi = c.at("Mhi", [P, KT, R], F32R, HID_OFF)
    c.Mlo = c.at("Mlo", [P, KT, R], F32R, HID_OFF + 33792)
    mixed = [c.mixA[:, k, :] for k in range(PAIRS)] + [c.y[:, k, :] for k in range(CT)]
    mix_hi, mix_lo, x_back = c.sem("mix_hi_ready"), c.sem("mix_lo_ready"), c.sem("x_back")
    c.Ahi2 = c.at("Ahi2", [P, KT, R], F32R, ACT_OFF)
    c.Alo2 = c.at("Alo2", [P, KT, R], F32R, ACT_OFF + 33792)
    c.sq = [c.at(f"sq{s}", [P, R], F32, SQ_OFF + 4224 * s) for s in range(2)]
    c.ssq = c.rstd
    c.zeros = c.eps
    W = Weights(c, "wo", RAW_OFF, 2, KT, KCS_OFF)
    N = NextNorm(c, "o", 1, W.free)
    heads = a["w_out"][0, 0:H * DH, :].rearrange("(e i d) n -> e d i n", e=KVH, d=DH)
    conv = a["w_out"][0, H * DH:, :].rearrange("(k p) n -> p k n", p=P)
    zeroed = c.sem("zeroed")
    with nc.psum_tensor("ps_w0", [P, NCH, 512], F32) as ps0, nc.psum_tensor("ps_w1", [P, NCH, 512], F32) as ps1, nc.Block() as block:
        ps = [ps0, ps1]

        def tiles(eng, body):
            rounds(eng, KT // 2, lambda r: [body(r * 2 + s, s) for s in range(2)])

        @block.sync
        def _(sp):
            def tile(t, s):
                n = ds(t * P, P)
                W.load(sp, t, s, [((slice(0, DH), slice(0, PAIRS)), heads[0, :, :, n]), ((slice(DH, P), slice(0, PAIRS)), heads[1, :, :, n]),
                                  ((slice(0, P), slice(PAIRS, KT)), conv[:, :, n])])
            tile(0, 0)
            tile(1, 1)
            sp.wait_ge(mix_lo, KT)
            sp.dma_start(c.xT[:, 0:CT, :].rearrange("p k r -> p (k r)"), c.x_spill[:, 0:CT * R]).then_inc(x_back, 16)
            with sp.Fori(1, KT // 2) as r:
                for s in range(2):
                    tile(r * 2 + s, s)

        @block.gpsimd
        def _(pool):
            nc.gpsimd.memset(c.zeros[:], 0.0).then_inc(zeroed, 1)
            pool.wait_ge(zeroed, 1)
            W.split_lo(pool, 0, 0)
            W.split_lo(pool, 1, 1)

            def pair(r):
                for s in range(2):
                    W.split_lo(pool, r * 2 + (2 + s), s)
                    N.pool(pool, r * 2 + s, s)
            rounds(pool, KT // 2 - 1, pair)
            for s in range(2):
                N.pool(pool, KT - 2 + s, s)

        @block.scalar
        def _(act):
            def split(k):
                nc.scalar.activation(c.Mhi[:, k, :], mixed[k], ACT.Copy).then_inc(mix_hi, 1)
            split(0)
            split(1)
            W.split_hi(act, 0, 0, 3)
            for k in range(2, KT):
                split(k)
            W.split_hi(act, 1, 1, 3)

            def pair(r):
                for s in range(2):
                    W.split_hi(act, r * 2 + (2 + s), s, 3)
                    N.act(act, r * 2 + s, s)
            rounds(act, KT // 2 - 1, pair)
            for s in range(2):
                N.act(act, KT - 2 + s, s)

        @block.tensor
        def _(pe):
            def tile(t, s):
                W.multiply(pe, t, s, ps[s], lambda k: c.Mhi[:, k, :], lambda k: c.Mlo[:, k, :],
                           before=(lambda k: pe.wait_ge(mix_lo, k + 1)) if isinstance(t, int) and t == 0 else None)
            tiles(pe, tile)

        @block.vector
        def _(dve):
            for k in range(KT):
                dve.wait_ge(mix_hi, k + 1)
                nc.vector.tensor_tensor(c.Mlo[:, k, :], mixed[k], c.Mhi[:, k, :].bitcast(F32), ALU.subtract).then_inc(mix_lo, 1)
            dve.wait_ge(x_back, 16)

            def tile(t, s):
                after(dve, W.done, t + 1)
                x = c.xT[:, ds(t, 1), :].rearrange("p o r -> p (o r)")
                nc.vector.tensor_tensor(three(x), ps[s][:, :, 0:CH], three(x), ALU.add).then_inc(W.free, 1)
                N.dve(dve, t, s)
            tiles(dve, tile)


def mlp(c):
    nc, a = c.nc, c.a
    inverse_rms(c, "n1", c.rstd)
    Hhi = c.at("Hhi", [P, 2, 4, R], F32R, HID_OFF)
    Hlo = c.at("Hlo", [P, 2, 4, R], F32R, HID_OFF + 33792)
    W = Weights(c, "wm", RAW_OFF, 2, KT, KCS_OFF)
    N = NextNorm(c, "m", 2, W.free, 12 * (FF // P // 4) - KT)
    up = a["w_up"].rearrange("o (k p) n -> p (o k) n", p=P)
    down = a["w_down"].rearrange("o (k p) n -> p (o k) n", p=P)
    NG = FF // P // 4
    sqd, h_hi, h_lo = c.sem("m_squared"), c.sem("m_hid_hi"), c.sem("m_hid_lo")

    def schedule(eng, ups, downs):
        for j in range(4):
            ups(j, j % 2, 0, 0, j)

        def step(t, i, slot):
            for j in range(4):
                ups(t + j, j % 2, i + 1, 1 - slot, j)
            for j in range(KT):
                downs(t + (4 + j), j % 2, i, slot, j, False)
        step(4, 0, 0)
        with eng.Fori(0, (NG - 2) // 2) as r:
            step(r * 24 + 16, r * 2 + 1, 1)
            step(r * 24 + 28, r * 2 + 2, 0)
        for j in range(KT):
            downs(12 * NG - 8 + j, j % 2, NG - 1, (NG - 1) % 2, j, True)

    with nc.psum_tensor("ps_m0", [P, NCH, 512], F32) as ps0, nc.psum_tensor("ps_m1", [P, NCH, 512], F32) as ps1, nc.Block() as block:
        ps = [ps0, ps1]
        half = (slice(0, P), slice(0, 4))

        @block.sync
        def _(sp):
            schedule(sp, lambda t, s, i, slot, j: W.load(sp, t, s, [((slice(0, P),), up[:, :, ds(i * 512 + P * j, P)])]),
                     lambda t, s, i, slot, j, last: W.load(sp, t, s, [(half, down[:, ds(i * 4, 4), P * j:P * j + P])]))

        @block.gpsimd
        def _(pool):
            def downs(t, s, i, slot, j, last):
                W.split_lo(pool, t, s, 4)
                if last and j >= 2:
                    N.pool(pool, j - 2, j % 2)
            schedule(pool, lambda t, s, i, slot, j: W.split_lo(pool, t, s), downs)
            N.pool(pool, KT - 2, 0)
            N.pool(pool, KT - 1, 1)

        @block.scalar
        def _(act):
            def hidden(t, s, slot, j, n):
                after(act, W.free, t + 1)
                nc.scalar.activation(c.sq[s][:], c.sq[s][:], ACT.Square).then_inc(sqd, 1)
                after(act, sqd, n + 1)
                nc.scalar.activation(Hhi[:, slot, j, :], c.sq[s][:], ACT.Copy).then_inc(h_hi, 1)

            for j in range(5):
                W.split_hi(act, j, j % 2, 1)
                if j:
                    hidden(j - 1, (j - 1) % 2, 0, j - 1, j - 1)

            def step(t, i, slot, first):
                for j in range(first, 4):
                    W.split_hi(act, t + j, j % 2, 1)
                    if j:
                        hidden(t + (j - 1), (j - 1) % 2, 1 - slot, j - 1, i * 4 + (j + 3))
                for j in range(KT):
                    W.split_hi(act, t + (4 + j), j % 2, 1, 4)
                    if j == 0:
                        hidden(t + 3, 1, 1 - slot, 3, i * 4 + 7)
            step(4, 0, 0, 1)
            with act.Fori(0, (NG - 2) // 2) as r:
                step(r * 24 + 16, r * 2 + 1, 1, 0)
                step(r * 24 + 28, r * 2 + 2, 0, 0)
            for j in range(KT):
                W.split_hi(act, 12 * NG - 8 + j, j % 2, 1, 4)
                if j >= 2:
                    N.act(act, j - 2, j % 2)
            N.act(act, KT - 2, 0)
            N.act(act, KT - 1, 1)

        @block.tensor
        def _(pe):
            def downs(t, s, i, slot, j, last):
                if j == 0:
                    after(pe, h_lo, i * 4 + 4)
                W.multiply(pe, t, s, ps[s], lambda k: Hhi[:, slot, k, :], lambda k: Hlo[:, slot, k, :], 4)
            schedule(pe, lambda t, s, i, slot, j: W.multiply(pe, t, s, ps[s], lambda k: c.Ahi2[:, k, :], lambda k: c.Alo2[:, k, :]), downs)

        @block.vector
        def _(dve):
            def ups(t, s, i, slot, j):
                n = i * 4 + j
                after(dve, W.done, t + 1)
                after(dve, h_lo, n - 1)
                nc.vector.scalar_tensor_tensor(out=three(c.sq[s][:]), in0=ps[s][:, :, 0:CH], scalar=0.0, in1=three(c.rstd[:]),
                                               op0=ALU.max, op1=ALU.mult).then_inc(W.free, 1)
                after(dve, h_hi, n + 1)
                nc.vector.tensor_tensor(Hlo[:, slot, j, :], c.sq[s][:], Hhi[:, slot, j, :].bitcast(F32), ALU.subtract).then_inc(h_lo, 1)

            def downs(t, s, i, slot, j, last):
                after(dve, W.done, t + 1)
                x = c.xT[:, j, :]
                after(dve, W.free, t - 11)
                nc.vector.tensor_tensor(three(x), ps[s][:, :, 0:CH], three(x), ALU.add).then_inc(W.free, 1)
                if last and j >= 1:
                    N.dve(dve, j - 1, (j - 1) % 2)
            schedule(dve, ups, downs)
            N.dve(dve, KT - 1, 1)


def layer_embedding(c):
    nc, a = c.nc, c.a
    rstd = c.at("rstd_ple", [P, R], F32, HID_OFF + 43264)
    inverse_rms(c, "n2", rstd)
    PK = PLE // P
    p_rows = c.at("p_rows", [P, QB + 1, PLE], F32, HID_OFF)
    pT = c.at("pT", [P, PK, R], F32, HID_OFF + 9216)
    Phi = c.at("Phi", [P, PK, R], F32R, HID_OFF + 17664)
    Plo = c.at("Plo", [P, PK, R], F32R, HID_OFF + 26112)
    sg = [c.at(f"ple_gate{s}", [P, R], F32, HID_OFF + 34816 + 4224 * s) for s in range(2)]
    W = Weights(c, "wg", RAW_OFF, 2, KT, KCS_OFF)
    x_added = c.sem("g_x_added")
    N = NextNorm(c, "g", 3, x_added, split=False)
    p_loaded, turned, kept, p_hi, p_lo = c.sem("p_loaded"), c.sem("p_rows_turned"), c.sem("p_kept"), c.sem("p_hi"), c.sem("p_lo")
    pre, sig = c.sem("g_pre"), c.sem("g_sigmoid")
    gate = a["w_ple_gate"].rearrange("o (k p) n -> p (o k) n", p=P)
    ple = a["w_ple"].rearrange("o (k p) n -> p (o k) n", p=P)
    with (nc.psum_tensor("ps_g0", [P, NCH, 512], F32) as ps0, nc.psum_tensor("ps_g1", [P, NCH, 512], F32) as ps1,
          nc.psum_tensor("ps_pt0", [P, 512], F32) as ps_pt0, nc.psum_tensor("ps_pt1", [P, 512], F32) as ps_pt1, nc.Block() as block):
        ps, ps_pt = [ps0, ps1], [ps_pt0, ps_pt1]

        @block.sync
        def _(sp):
            sp.dma_start(p_rows[:, 0:QB, :], a["p_prompt"].rearrange("o b (r p) f -> p (o b r) f", p=P)).then_inc(p_loaded, 16)
            sp.dma_start(p_rows[0:SR, QB, :], a["p_sample"].rearrange("o b t f -> (o b t) f")).then_inc(p_loaded, 16)

            def pair(r):
                W.load(sp, r * 2, 0, [((slice(0, P),), gate[:, :, ds(r * P, P)])])
                W.load(sp, r * 2 + 1, 1, [((slice(0, P), slice(0, PK)), ple[:, :, ds(r * P, P)])])
            rounds(sp, KT, pair)

        @block.tensor
        def _(pe):
            pe.wait_ge(p_loaded, 32)
            for r in range(QB + 1):
                n = P if r < QB else SR
                if r >= 2:
                    pe.wait_ge(kept, r - 1)
                for k in range(PK):
                    mm = nc.tensor.transpose(ps_pt[r % 2][:, n * k:n * k + n], p_rows[0:n, r, P * k:P * k + P], c.ident[0:n, 0:n])
                mm.then_inc(turned, 1)

            def pair(r):
                W.multiply(pe, r * 2, 0, ps[0], lambda k: c.Ahi2[:, k, :], lambda k: c.Alo2[:, k, :])
                if isinstance(r, int):
                    pe.wait_ge(p_lo, 1)
                W.multiply(pe, r * 2 + 1, 1, ps[1], lambda k: Phi[:, k, :], lambda k: Plo[:, k, :], PK)
            rounds(pe, KT, pair)

        @block.gpsimd
        def _(pool):
            def pair(r):
                W.split_lo(pool, r * 2, 0)
                W.split_lo(pool, r * 2 + 1, 1, PK)
            pair(0)
            pair(1)
            N.pool(pool, 0, 0)
            pair(2)
            N.pool(pool, 1, 1)
            with pool.Fori(1, KT // 2 - 1) as r:
                pair(r * 2 + 1)
                N.pool(pool, r * 2, 0)
                pair(r * 2 + 2)
                N.pool(pool, r * 2 + 1, 1)
            pair(KT - 1)
            N.pool(pool, KT - 2, 0)
            N.pool(pool, KT - 1, 1)

        @block.scalar
        def _(act):
            def splits(r):
                W.split_hi(act, r * 2, 0, 1)
                W.split_hi(act, r * 2 + 1, 1, 1, PK)

            def work(r, s):
                after(act, pre, r + 1)
                nc.scalar.activation(sg[s][:], sg[s][:], ACT.Sigmoid).then_inc(sig, 1)
                N.act(act, r, s)
            splits(0)
            act.wait_ge(kept, QB + 1)
            nc.scalar.activation(Phi[:], pT[:], ACT.Copy).then_inc(p_hi, 1)
            splits(1)
            work(0, 0)
            splits(2)
            work(1, 1)
            with act.Fori(1, KT // 2 - 1) as r:
                splits(r * 2 + 1)
                work(r * 2, 0)
                splits(r * 2 + 2)
                work(r * 2 + 1, 1)
            splits(KT - 1)
            work(KT - 2, 0)
            work(KT - 1, 1)

        @block.vector
        def _(dve):
            for r in range(QB + 1):
                n = P if r < QB else SR
                dve.wait_ge(turned, r + 1)
                nc.vector.tensor_copy(pT[:, :, P * r:P * r + n], ps_pt[r % 2][:, 0:PK * n].rearrange("p (k n) -> p k n", n=n)).then_inc(kept, 1)
            dve.wait_ge(p_hi, 1)
            nc.vector.tensor_tensor(Plo[:], pT[:], Phi[:].bitcast(F32), ALU.subtract).then_inc(p_lo, 1)

            def pair(r, s):
                after(dve, W.done, r * 2 + 1)
                nc.vector.tensor_tensor(three(sg[s][:]), ps[0][:, :, 0:CH], three(rstd[:]), ALU.mult).then_inc(pre, 1)
                after(dve, sig, r + 1)
                after(dve, W.done, r * 2 + 2)
                nc.vector.tensor_tensor(three(sg[s][:]), ps[1][:, :, 0:CH], three(sg[s][:]), ALU.mult).then_inc(W.free, 2)
                after(dve, W.free, r * 2 + 2)
                x = c.xT[:, ds(r, 1), :].rearrange("p o r -> p (o r)")
                nc.vector.tensor_tensor(x, x, sg[s][:], ALU.add).then_inc(x_added, 1)
            rounds(dve, KT // 2, lambda r: [pair(r * 2 + s, s) for s in range(2)])


def finish(c):
    nc, a = c.nc, c.a
    inverse_rms(c, "n3", c.rstd)
    rows = [c.at(f"y_rows{s}", [P, D], F32, HID_OFF + 4096 * s) for s in range(3)]
    ready, turned, kept_a, kept_v = c.sem("f_ready"), c.sem("f_turned"), c.sem("f_kept_act"), c.sem("f_kept_dve")
    out = [c.sem(f"f_out{s}") for s in range(3)]
    NR = QB + 1
    with nc.psum_tensor("ps_f4", [P, 4, 512], F32) as ps, nc.Block() as block:
        def n_rows(r):
            return P if r < QB else SR

        @block.vector
        def _(dve):
            for k in range(KT):
                nc.vector.scalar_tensor_tensor(out=c.xT[:, k, :], in0=c.xT[:, k, :], scalar=c.gains[:, 3, k:k + 1], in1=c.rstd[:],
                                               op0=ALU.mult, op1=ALU.mult).then_inc(ready, 1)
            for r in range(NR):
                n = n_rows(r)
                dve.wait_ge(turned, 2 * r + 2)
                if r >= 3:
                    dve.wait_ge(out[r % 3], 16 * (r // 3))
                nc.vector.tensor_copy(rows[r % 3][0:n, 512:1024], ps[0:n, 2 * (r % 2) + 1, :]).then_inc(kept_v, 1)

        @block.scalar
        def _(act):
            for r in range(NR):
                n = n_rows(r)
                act.wait_ge(turned, 2 * r + 1)
                if r >= 3:
                    act.wait_ge(out[r % 3], 16 * (r // 3))
                nc.scalar.activation(rows[r % 3][0:n, 0:512], ps[0:n, 2 * (r % 2), :], ACT.Copy).then_inc(kept_a, 1)

        @block.tensor
        def _(pe):
            pe.wait_ge(ready, KT)
            for r in range(NR):
                n = n_rows(r)
                for half in range(2):
                    if r >= 2:
                        pe.wait_ge((kept_a, kept_v)[half], r - 1)
                    for k in range(4):
                        mm = nc.tensor.transpose(ps[0:n, 2 * (r % 2) + half, P * k:P * k + P], c.xT[:, 4 * half + k, P * r:P * r + n], c.ident[:])
                    mm.then_inc(turned, 1)

        @block.sync
        def _(sp):
            for r in range(NR):
                sp.wait_ge(kept_a, r + 1)
                sp.wait_ge(kept_v, r + 1)
                dst = a["y_prompt"][0, P * r:P * r + P, :] if r < QB else a["y_sample"].rearrange("b t f -> (b t) f")
                sp.dma_start(dst, rows[r % 3][0:n_rows(r), :]).then_inc(out[r % 3], 16)
            for s in range(3):
                sp.wait_ge(out[s], 48)
            sp.wait_ge(c.stored, c.n_stored)


INPUTS = ("x_prompt", "x_sample", "p_prompt", "p_sample", "cache_cmp_kv", "cache_slc_kv", "cache_win_kv", "state_conv",
          "page_table", "g_attn", "w_in", "w_cmp1", "w_cmp2", "pe_cmp", "conv_w", "conv_b", "ln_conv_g", "ln_conv_b",
          "w_out", "g_mlp", "w_up", "w_down", "g_ple", "w_ple", "w_ple_gate", "g_final")
OUTPUTS = (("y_prompt", (1, T, D)), ("y_sample", (B, NEW, D)),
           ("prompt_cmp", (1, 1, T, 2, KVH, DH)), ("prompt_slc", (1, 1, T, 2, KVH, DH)),
           ("prompt_win", (1, 1, WIN, 2, KVH, DH)), ("prompt_conv", (1, 1, HIST, C)),
           ("sample_cmp", (1, B, NEW, 2, KVH, DH)), ("sample_slc", (1, B, NEW, 2, KVH, DH)),
           ("sample_win", (1, B, WIN, 2, KVH, DH)), ("sample_conv", (1, B, HIST, C)))


def kernel(**inputs):
    import numpy as _np
    import concourse.bacc as _bacc
    from concourse import mybir as _mybir
    from concourse.bass_utils import run_bass_kernel_spmd as _run

    nc = _bacc.Bacc("TRN2", target_bir_lowering=False, num_devices=1)
    arrays, tensors = {}, {}
    for name in INPUTS:
        x = _np.ascontiguousarray(inputs[name])
        arrays[f"in_{name}_dram"] = x
        tensors[name] = nc.dram_tensor(f"in_{name}_dram", x.shape, _mybir.dt.from_np(x.dtype), kind="ExternalInput").ap()
    for name, shape in OUTPUTS:
        tensors[name] = nc.dram_tensor(f"out_{name}_dram", shape, _mybir.dt.float32, kind="ExternalOutput").ap()
    build_program(nc, tensors)
    r = _run(nc, [arrays], core_ids=[0])
    return tuple(r.results[0][f"out_{name}_dram"] for name, _ in OUTPUTS)
```
